# Optimizing a Trainium2 kernel written in Bass

```python
import math
import jax
import jax.numpy as jnp
from jax import lax
import numpy as np

D_MODEL = 1024
BATCH = 1
SEQ = 1024
DEPTH = 1

EPS = 1e-6
A_HEADS = 8
A_LAT = 128
A_VDIM = 64
IDX_HEADS = 4
IDX_DIM = 64
IDX_TOPK_MAX = 256
Q_BLOCK = 128
B_HEADS = 4
B_DIM = 128
CONV_W = 4
CHUNK = 64
PEER_HEADS = 8
PEER_NKEYS = 128
PEER_QDIM = 256
PEER_TOPK = 16
PEER_BLOCK = 128
N_EXPERTS = PEER_NKEYS * PEER_NKEYS

A_WIDTH = A_HEADS * A_VDIM
B_WIDTH = B_HEADS * B_DIM
MIX_WIDTH = A_WIDTH + B_WIDTH
IN_SPLITS = (A_HEADS * A_LAT, A_LAT, IDX_HEADS * IDX_DIM, IDX_DIM, IDX_HEADS,
             B_WIDTH, B_WIDTH, B_WIDTH, B_WIDTH, B_HEADS, B_HEADS)
IN_WIDTH = sum(IN_SPLITS)

kernel_name = 'hybrid_dsa_gdn_peer_adaln_layer'

def rms(x):
    xf = x.astype(jnp.float32)
    return xf * lax.rsqrt(jnp.mean(xf * xf, -1, keepdims=True) + EPS)

def l2n(x):
    return x * lax.rsqrt(jnp.sum(x * x, -1, keepdims=True) + EPS)

def modulate(xn, shift, scale):
    return xn * (1.0 + scale[:, None, :]) + shift[:, None, :]

def causal_dwconv(x, w):
    C = x.shape[-1]
    return lax.conv_general_dilated(
        x, w[:, None, :].astype(x.dtype), window_strides=(1,),
        padding=[(w.shape[0] - 1, 0)], dimension_numbers=('NWC', 'WIO', 'NWC'),
        feature_group_count=C)

def dsa_attention(q_lat, kv, iq, ik, iw, q_gain, k_gain, w_uv):
    B, S = kv.shape[:2]
    topk = min(IDX_TOPK_MAX, S // 4)
    q = rms(q_lat) * q_gain
    k = rms(kv) * k_gain
    slopes = jnp.exp2(-8.0 * jnp.arange(1, A_HEADS + 1, dtype=jnp.float32) / A_HEADS)
    nb = S // Q_BLOCK
    key_pos = jnp.arange(S)
    scale = A_LAT ** -0.5
    idx_scale = (IDX_DIM ** -0.5) * (IDX_HEADS ** -0.5)

    def blocks(a):
        return a.reshape((B, nb, Q_BLOCK) + a.shape[2:]).swapaxes(0, 1)

    def one_block(args):
        qb, iqb, iwb, start = args
        qpos = start + jnp.arange(Q_BLOCK)
        causal = key_pos[None, :] <= qpos[:, None]
        logits = jnp.einsum('bqhd,bsd->bqhs', iqb, ik)
        score = jnp.einsum('bqhs,bqh->bqs', jax.nn.relu(logits), iwb).astype(jnp.float32) * idx_scale
        score = jnp.where(causal[None], score, -jnp.inf)
        _, sel = lax.top_k(score, topk)
        kv_sel = jax.vmap(lambda kb, ib: kb[ib])(k, sel)
        s = jnp.einsum('bqhr,bqkr->bqhk', qb, kv_sel) * scale
        dist = (qpos[None, :, None] - sel).astype(jnp.float32)
        s = s - slopes[None, None, :, None] * dist[:, :, None, :]
        valid = (sel <= qpos[None, :, None])[:, :, None, :]
        p = jax.nn.softmax(jnp.where(valid, s, -jnp.inf), axis=-1)
        return jnp.einsum('bqhk,bqkr->bqhr', p, kv_sel)

    starts = jnp.arange(nb, dtype=jnp.int32) * Q_BLOCK
    o = lax.map(one_block, (blocks(q), blocks(iq), blocks(iw), starts))
    o = o.swapaxes(0, 1).reshape(B, S, A_HEADS, A_LAT)
    return jnp.einsum('bshr,hrv->bshv', o, w_uv).reshape(B, S, A_WIDTH)

def gated_deltanet(q, k, v, z, a, b, conv_w, a_log, dt_bias, norm_gain):
    B, S = q.shape[:2]
    qkv = jax.nn.silu(causal_dwconv(jnp.concatenate([q, k, v], -1), conv_w)).astype(jnp.float32)
    q, k, v = jnp.split(qkv, 3, axis=-1)

    def heads(t):
        return t.reshape(B, S, B_HEADS, B_DIM).transpose(0, 2, 1, 3)

    q = l2n(heads(q)) * (B_DIM ** -0.5)
    k = l2n(heads(k))
    v = heads(v)
    beta = jax.nn.sigmoid(b.astype(jnp.float32)).transpose(0, 2, 1)
    g = (-jnp.exp(a_log.astype(jnp.float32))
         * jax.nn.softplus(a.astype(jnp.float32) + dt_bias.astype(jnp.float32))).transpose(0, 2, 1)
    n = S // CHUNK

    def chunks(t):
        return t.reshape(t.shape[:2] + (n, CHUNK) + t.shape[3:])

    q, k, v, beta, g = (chunks(t) for t in (q, k, v, beta, g))
    G = jnp.cumsum(g, axis=-1)
    tril = jnp.tril(jnp.ones((CHUNK, CHUNK), bool))
    strict = jnp.tril(jnp.ones((CHUNK, CHUNK), bool), -1)
    decay = jnp.exp(jnp.where(tril, G[..., :, None] - G[..., None, :], -jnp.inf))
    kb = k * beta[..., None]
    Lmat = jnp.where(strict, jnp.einsum('bhnid,bhnjd->bhnij', kb, k) * decay, 0.0)
    eye = jnp.eye(CHUNK, dtype=jnp.float32)
    T = lax.linalg.triangular_solve(eye + Lmat, jnp.broadcast_to(eye, Lmat.shape),
                                    left_side=True, lower=True, unit_diagonal=True)
    u = T @ (v * beta[..., None])
    w = T @ (kb * jnp.exp(G)[..., None])
    attn_intra = jnp.einsum('bhnid,bhnjd->bhnij', q, k) * decay
    q_dec = q * jnp.exp(G)[..., None]
    k_dec = k * jnp.exp(G[..., -1:] - G)[..., None]
    g_last = jnp.exp(G[..., -1])

    def step(state, xs):
        u_c, w_c, a_c, qd_c, kd_c, gl_c = xs
        v_new = u_c - jnp.einsum('bhck,bhkv->bhcv', w_c, state)
        o = jnp.einsum('bhck,bhkv->bhcv', qd_c, state) + jnp.einsum('bhij,bhjv->bhiv', a_c, v_new)
        state = state * gl_c[..., None, None] + jnp.einsum('bhck,bhcv->bhkv', kd_c, v_new)
        return state, o

    xs = tuple(jnp.moveaxis(t, 2, 0) for t in (u, w, attn_intra, q_dec, k_dec, g_last))
    state0 = jnp.zeros((B, B_HEADS, B_DIM, B_DIM), jnp.float32)
    _, o = lax.scan(step, state0, xs)
    o = jnp.moveaxis(o, 0, 2).reshape(B, B_HEADS, S, B_DIM).transpose(0, 2, 1, 3)
    zh = z.reshape(B, S, B_HEADS, B_DIM).astype(jnp.float32)
    o = rms(o) * norm_gain * jax.nn.silu(zh)
    return o.reshape(B, S, B_WIDTH)

def peer(h, w_query, sub_keys, u_tab, v_tab):
    B, S, D = h.shape
    hb_all = h.reshape(-1, PEER_BLOCK, D)

    def one_block(hb):
        q = (hb @ w_query).reshape(PEER_BLOCK, PEER_HEADS, 2, PEER_QDIM // 2)
        s = jnp.einsum('thpd,hpnd->thpn', q, sub_keys).astype(jnp.float32)
        s_half, i_half = lax.top_k(s, PEER_TOPK)
        cand = s_half[..., 0, :, None] + s_half[..., 1, None, :]
        cand_s, cand_i = lax.top_k(cand.reshape(PEER_BLOCK, PEER_HEADS, PEER_TOPK * PEER_TOPK), PEER_TOPK)
        i1 = jnp.take_along_axis(i_half[..., 0, :], cand_i // PEER_TOPK, axis=-1)
        i2 = jnp.take_along_axis(i_half[..., 1, :], cand_i % PEER_TOPK, axis=-1)
        expert = i1 * PEER_NKEYS + i2
        gate = jax.nn.softmax(cand_s, axis=-1)
        act = jax.nn.gelu(jnp.einsum('tpkd,td->tpk', u_tab[expert], hb).astype(jnp.float32),
                          approximate=False) * gate
        return jnp.einsum('tpk,tpkd->td', act.astype(v_tab.dtype), v_tab[expert])

    return lax.map(one_block, hb_all).reshape(B, S, D)

def setup_inputs(seed: int = 0) -> dict:
    key = jax.random.key(seed)
    ks = jax.random.split(key, 18)
    f32 = jnp.float32
    L = DEPTH

    def nrm(k, shape, fan_in, gain=1.0):
        return jax.random.normal(k, shape, f32) * (gain * fan_in ** -0.5)

    dt = jnp.exp(jax.random.uniform(ks[10], (L, B_HEADS), f32,
                                    minval=math.log(1e-3), maxval=math.log(1e-1)))
    return {
        'x': jax.random.normal(ks[0], (BATCH, SEQ, D_MODEL), f32),
        'c': jax.random.normal(ks[1], (BATCH, D_MODEL), f32),
        'w_ada': nrm(ks[2], (L, D_MODEL, 6 * D_MODEL), D_MODEL, 0.5),
        'b_ada': 0.02 * jax.random.normal(ks[3], (L, 6 * D_MODEL), f32),
        'w_in': nrm(ks[4], (L, D_MODEL, IN_WIDTH), D_MODEL),
        'q_gain': 1.0 + 0.02 * jax.random.normal(ks[5], (L, A_LAT), f32),
        'k_gain': 1.0 + 0.02 * jax.random.normal(ks[6], (L, A_LAT), f32),
        'w_uv': nrm(ks[7], (L, A_HEADS, A_LAT, A_VDIM), A_LAT),
        'conv_w': nrm(ks[8], (L, CONV_W, 3 * B_WIDTH), CONV_W),
        'a_log': jnp.log(jax.random.uniform(ks[9], (L, B_HEADS), f32, minval=1.0, maxval=16.0)),
        'dt_bias': dt + jnp.log(-jnp.expm1(-dt)),
        'gdn_gain': 1.0 + 0.02 * jax.random.normal(ks[11], (L, B_DIM), f32),
        'w_out': nrm(ks[12], (L, MIX_WIDTH, D_MODEL), MIX_WIDTH),
        'w_query': nrm(ks[13], (L, D_MODEL, PEER_HEADS * PEER_QDIM), D_MODEL),
        'sub_keys': nrm(ks[14], (L, PEER_HEADS, 2, PEER_NKEYS, PEER_QDIM // 2), PEER_QDIM // 2),
        'u_tab': nrm(ks[15], (L, N_EXPERTS, D_MODEL), D_MODEL),
        'v_tab': nrm(ks[16], (L, N_EXPERTS, D_MODEL), D_MODEL),
    }

def reference(x, c, w_ada, b_ada, w_in, q_gain, k_gain, w_uv, conv_w, a_log, dt_bias,
              gdn_gain, w_out, w_query, sub_keys, u_tab, v_tab):
    B, S, _ = x.shape
    offsets = [int(o) for o in np.cumsum(IN_SPLITS)[:-1]]
    for l in range(DEPTH):
        sh1, sc1, g1, sh2, sc2, g2 = jnp.split(jax.nn.silu(c) @ w_ada[l] + b_ada[l], 6, axis=-1)
        h = modulate(rms(x), sh1, sc1).astype(x.dtype)
        proj = h @ w_in[l]
        aq, akv, iq, ik, iw, bq, bk, bv, bz, ba, bb = jnp.split(proj, offsets, axis=-1)
        ya = dsa_attention(aq.reshape(B, S, A_HEADS, A_LAT), akv,
                           iq.reshape(B, S, IDX_HEADS, IDX_DIM), ik, iw,
                           q_gain[l], k_gain[l], w_uv[l])
        yb = gated_deltanet(bq, bk, bv, bz, ba, bb, conv_w[l], a_log[l], dt_bias[l], gdn_gain[l])
        mix = jnp.concatenate([ya, yb], axis=-1).astype(x.dtype) @ w_out[l]
        x = x + (g1[:, None, :] * mix).astype(x.dtype)
        h = modulate(rms(x), sh2, sc2).astype(x.dtype)
        y = peer(h, w_query[l], sub_keys[l], u_tab[l], v_tab[l])
        x = x + (g2[:, None, :] * y).astype(x.dtype)
    return x


_drawn_inputs = setup_inputs


def setup_inputs(seed=0):
    import zlib

    import numpy as np

    out = dict(_drawn_inputs(seed))
    spreads = {}
    factors = {'b_ada': 2.715,
     'q_gain': 8.0,
     'k_gain': 8.0,
     'a_log': 2.878,
     'gdn_gain': 8.0,
     'w_query': 8.0,
     'sub_keys': 8.0,
     'u_tab': 8.0,
     'v_tab': 8.0}
    for name, (base, spread) in spreads.items():
        noise = np.random.default_rng([zlib.crc32(name.encode()), seed]).standard_normal(out[name].shape)
        drawn = base * np.exp(spread * noise) if base else spread * noise
        out[name] = jnp.asarray(drawn.astype(out[name].dtype))
    for name, factor in factors.items():
        out[name] = (out[name] * factor).astype(out[name].dtype)
    return out
```

```python
from contextlib import ExitStack

import numpy as np

import concourse.bass as bass
from concourse import mybir

F32 = mybir.dt.float32
BF16 = mybir.dt.bfloat16
U32 = mybir.dt.uint32
ALU = mybir.AluOpType
ACT = mybir.ActivationFunctionType
AX = mybir.AxisListType

P = 128
S = 1024
D = 1024
NT = S // P
KC = D // P
HALF = 512
EPS = 1e-6
A_HEADS, A_LAT, A_VDIM = 8, 128, 64
IDX_HEADS, IDX_DIM, TOPK = 4, 64, 256
B_HEADS, B_DIM, CONV_W = 4, 128, 4
PEER_HEADS, NKEYS, PEER_TOPK = 8, 128, 16
SPLITS = (A_HEADS * A_LAT, A_LAT, IDX_HEADS * IDX_DIM, IDX_DIM, IDX_HEADS,
          B_HEADS * B_DIM, B_HEADS * B_DIM, B_HEADS * B_DIM, B_HEADS * B_DIM, B_HEADS, B_HEADS)
(AQ, AKV, IQ, IK, IW, BQ, BK, BV, BZ, BA, BB) = (int(o) for o in np.cumsum((0,) + SPLITS[:-1]))
MASKED = -1e30
TAKEN = -3e38
ATT_SCALE = A_LAT ** -0.5
IDX_SCALE = IDX_DIM ** -0.5 * IDX_HEADS ** -0.5
SLOPES = [2.0 ** (-8.0 * (h + 1) / A_HEADS) for h in range(A_HEADS)]
QBS = list(range(NT - 1, 1, -1))
LEVELS = 7
G_TOK = 64
G_BLOCKS = S // G_TOK
SG = 4
NSG = NKEYS // SG
POOL_CONSTS = 12 + 3 * LEVELS


def weight_segments(w_ada, w_in, w_out, w_query):
    def cols(w, lo, n):
        return w.rearrange("(kc p) n -> p kc n", p=P)[:, :, lo:lo + n]

    def ada(part):
        return [[(0, cols(w_ada, part * D + i * HALF, HALF))] for i in range(2)]

    def whole(w, lo, n):
        return [[(0, cols(w, lo + i * HALF, HALF))] for i in range(n // HALF)]

    segs, first = [], {}

    def add(name, more):
        first[name] = len(segs)
        segs.extend(more)

    add("scale1", ada(1))
    add("shift1", ada(0))
    add("index", [[(0, cols(w_in, IQ, 256)), (256, cols(w_in, IK, 64)), (320, cols(w_in, IK, 64))]])
    add("small", [[(0, cols(w_in, AKV, 128)), (128, cols(w_in, IW, 4)), (132, cols(w_in, BA, 8))]])
    add("qkv", whole(w_in, BQ, 3 * HALF))
    add("z", whole(w_in, BZ, HALF))
    add("aq", whole(w_in, AQ, 2 * HALF))
    add("gate1", ada(2))
    add("out", whole(w_out, 0, D))
    add("scale2", ada(4))
    add("shift2", ada(3))
    add("query", whole(w_query, 0, 4 * HALF))
    add("gate2", ada(5))
    return segs, first


def layer(nc, x, c_col, w_ada, b_col, b_gate, w_in, q_gain_col, k_gain, w_uv, conv_col, a_log,
          dt_bias, gdn_gain, w_out, w_query, subT, uT, v_tab, out):
    with ExitStack() as ctx:
        def sem(name):
            return ctx.enter_context(nc.semaphore(name))

        def sb(name, shape, dt=F32):
            return ctx.enter_context(nc.sbuf_tensor(name, shape, dt))

        aq_dram = nc.dram_tensor("aq_spill", [S, D], F32).ap()
        x1_dram = nc.dram_tensor("x1_spill", [S, D], F32).ap()
        g_dram = nc.dram_tensor("gates", [G_BLOCKS, P, NKEYS, G_TOK], F32).ap()

        pair = [ctx.enter_context(nc.psum_tensor(f"pair{i}", [P, 2 * HALF], F32)) for i in range(4)]

        def bank(i):
            return pair[i // 2][:, (i % 2) * HALF:(i % 2 + 1) * HALF]

        ident = sb("ident", [P, P])
        ones = sb("ones", [P, P])
        triu = sb("triu", [P, P])
        causal = sb("causal", [P, P])
        level = sb("level", [P, LEVELS, P])
        iota_c = sb("iota_c", [P, P])
        dist = sb("dist", [P, S])
        eps = sb("eps", [P, 2])
        c_sb = sb("c_sb", [P, KC])
        c_rep = sb("c_rep", [P, KC, P])
        mods = sb("mods", [P, 4, KC])
        b_sb = sb("b_sb", [P, 48])
        st = sb("st", [P, 8, 16])
        qg = sb("qg", [P, 1])
        kg = sb("kg", [P, A_LAT])
        gg = sb("gg", [P, B_DIM])
        conv_sb = sb("conv_sb", [P, 12, CONV_W])
        al = sb("al", [P, B_HEADS])
        dtb = sb("dtb", [P, B_HEADS])
        wuv = sb("wuv", [P, A_HEADS, A_VDIM])
        NARENA = (nc.sbuf_bytes_remaining - 256) // 4
        NARENA -= NARENA % 8
        arena = sb("arena", [P, NARENA])

        class Region:
            def __init__(self, start):
                self.at = start

            def take(self, *shape, dt=F32):
                n = int(np.prod(shape))
                words = n if dt in (F32, U32) else n // 2
                v = arena[:, self.at:self.at + words]
                self.at += words
                assert self.at <= NARENA, (self.at, NARENA)
                if dt is not F32:
                    v = v.bitcast(dt)
                if len(shape) == 2:
                    return v.rearrange("p (a b) -> p a b", a=shape[0])
                if len(shape) == 3:
                    return v.rearrange("p (a b c) -> p a b c", a=shape[0], b=shape[1])
                return v

        base = Region(0)
        hT = base.take(KC, S)
        mixT = hT
        wring = [base.take(KC, HALF) for _ in range(2)]
        R0 = base.at
        r = Region(R0)
        xbuf = r.take(NT, D)
        yacc = xbuf
        h2T = r.take(KC, S)
        R2 = r.at
        r = Region(R0)
        raw = r.take(12, CONV_W - 1 + S)
        z = r.take(NT, B_HEADS * B_DIM)
        small = r.take(NT, 140)
        MOFF = [P * qb * (qb + 1) // 2 for qb in range(NT + 1)]
        mask = r.take(MOFF[NT], dt=BF16)
        R3 = r.at
        iqT = r.take(3, S)
        aq_stage = [r.take(HALF) for _ in range(2)]
        relu = [r.take(S) for _ in range(2)]
        weighed = r.take(S)
        score = [r.take(S) for _ in range(2)]
        top8 = r.take(8)
        iw_s = r.take(NT, IDX_HEADS)
        r = Region(R3)
        HP = B_HEADS * P
        cv = [r.take(S) for _ in range(2)]
        norm = cv
        gates = r.take(16, NT * B_HEADS)
        spread = r.take(2, HP)
        grow, decayT = cv[0][:, 0:HP], cv[0][:, HP:2 * HP]
        attnT = r.take(HP)
        upper = r.take(HP)
        upper_s = [r.take(HP) for _ in range(2)]
        n1 = r.take(HP)
        inv = r.take(2, HP)
        kdec = r.take(HP)
        bv = r.take(HP)
        state = r.take(HP)
        resid = r.take(HP)
        vnew = r.take(HP)
        qse = r.take(HP)
        o_sb = r.take(HP)
        sqj, yb = cv[1][:, 0:HP], cv[1][:, HP:2 * HP]
        ost = r.take(4, B_HEADS)
        r = Region(R3)
        ktok = r.take(NT, A_LAT)
        kT = r.take(S)
        kst = r.take(4, NT)
        aqt = [r.take(A_HEADS, A_LAT) for _ in range(2)]
        qst = r.take(4, A_HEADS)
        sq_junk = r.take(A_LAT)
        r = Region(R0)
        qT = r.take(A_HEADS, P)
        dm = r.take(S)
        bias = [r.take(S) for _ in range(2)]
        sc = [r.take(S) for _ in range(2)]
        pr = [r.take(S) for _ in range(2)]
        smax = r.take(3, A_HEADS)
        PT = r.take(NT, 4, P)
        oT = r.take(A_HEADS, P)
        ya = r.take(A_HEADS * A_VDIM)
        r = Region(R2)
        grow1 = r.take(D)
        grow2 = r.take(D)
        bg = r.take(2, D)
        gmix = [Region(R2 + 4 * D).take(HALF), Region(R2 + 4 * D + HALF).take(HALF)]
        R4 = r.at
        pqT = [r.take(4, S) for _ in range(1)]
        sub = r.take(16, NKEYS)
        s_st = [r.take(HALF) for _ in range(2)]
        s_tmp = r.take(P)
        sh = r.take(NT, 16, PEER_TOPK)
        ih = r.take(NT, 16, PEER_TOPK)
        m_ix = r.take(4 * PEER_TOPK, dt=U32)
        r2 = Region(0)
        cand = r2.take(PEER_HEADS, 256)
        cand2 = r2.take(256)
        eq = r2.take(PEER_HEADS, PEER_TOPK, PEER_TOPK)
        cs = r2.take(PEER_HEADS, PEER_TOPK)
        ce = r2.take(PEER_HEADS, PEER_TOPK)
        ci = r2.take(PEER_HEADS * PEER_TOPK, dt=U32)
        cab = r2.take(2, PEER_HEADS * PEER_TOPK, dt=U32)
        cabf = r2.take(2, PEER_HEADS * PEER_TOPK)
        sel = [r2.take(3, PEER_HEADS * PEER_TOPK) for _ in range(2)]
        gs = r2.take(PEER_HEADS)
        assert r2.at <= R0 - KC * HALF * 2
        r = Region(R4 + 8)
        selT = r.take(3, S)
        oh1 = r.take(8, P)
        oh2 = r.take(8, P)
        gst = [Region(i * NKEYS * G_TOK).take(NKEYS, G_TOK) for i in range(2)]
        r = Region(0)
        actT = [r.take(SG, S) for _ in range(2)]
        v_sb = [r.take(SG, D) for _ in range(2)]
        assert r.at <= R0
        r = Region(R2 + 2 * D)
        u_sb = [r.take(KC, P) for _ in range(SG)]
        g_sb = [r.take(G_BLOCKS, SG, G_TOK) for _ in range(2)]
        x1_in_sb = Region(0).take(NT, D)

        segs, seg0 = weight_segments(w_ada, w_in, w_out, w_query)
        NSEG = len(segs)

        consts_in = sem("consts_in")
        x_in = [sem(f"x_in{i}") for i in range(2)]
        x2_in = sem("x2_in")
        w_in_s = [sem(f"w_slot{i}") for i in range(2)]
        pool_const = sem("pool_const")
        silu_c = sem("silu_c")
        c_wide = sem("c_wide")
        ada_mm = sem("ada_mm")
        ada_row = sem("ada_row")
        mods_done = sem("mods_done")
        sq_done = sem("sq_done")
        ms_done = sem("ms_done")
        rt_done = sem("rt_done")
        dve_c = sem("dve_c")
        act_c = sem("act_c")
        pool_c = sem("pool_c")
        xn_done = sem("xn_done")
        hx_mm = sem("hx_mm")
        hx_act = sem("hx_act")
        hx_dve = sem("hx_dve")
        proj_mm = sem("proj_mm")
        proj_out = sem("proj_out")
        aq_out = [sem(f"aq_out{i}") for i in range(2)]
        raw_pad = sem("raw_pad")
        idx_mm = sem("idx_mm")
        idx_relu = sem("idx_relu")
        idx_acc = sem("idx_acc")
        score_done = sem("score_done")
        iws_done = sem("iws_done")
        topk_done = sem("topk_done")

        SEG_SMALL = seg0["small"]
        jobs = [("index", seg0["index"], f, h) for f in range(3) for h in range(2)]
        jobs += [("small", SEG_SMALL, t, 0) for t in range(NT)]
        N_SMALL = len(jobs)
        jobs += [("qkv", seg0["qkv"] + j // 4, j, h) for j in range(12) for h in range(2)]
        N_QKV = len(jobs)
        jobs += [("z", seg0["z"], t, 0) for t in range(NT)]
        jobs += [("aq", seg0["aq"] + i, t, i) for i in range(2) for t in range(NT)]
        IDX_AT = [N_SMALL, N_SMALL, N_SMALL + 12, N_SMALL + 22, N_SMALL + 30, N_SMALL + 38]
        last_of = {}
        for n, job in enumerate(jobs):
            last_of[job[1]] = n + 1

        released = {}
        for name, n0 in (("scale1", 0), ("shift1", 2), ("gate1", 4), ("scale2", 6), ("shift2", 8), ("gate2", 10)):
            for i in range(2):
                released[seg0[name] + i] = (ada_mm, n0 + i + 1)
        for s_, n in last_of.items():
            released[s_] = (proj_mm, n)
        out_mm = sem("out_mm")
        q_mm = sem("q_mm")
        for i in range(2):
            released[seg0["out"] + i] = (out_mm, NT * (i + 1))
        for i in range(4):
            released[seg0["query"] + i] = (q_mm, 8 * (i + 1))

        slot_uses = [0, 0]
        seg_ready = []
        for n, parts in enumerate(segs):
            slot_uses[n % 2] += 16 * len(parts)
            seg_ready.append(slot_uses[n % 2])

        class Steps:
            def __init__(self, eng, s_):
                self.eng, self.sem, self.n = eng, s_, 0
                self.before, self.first = None, 0

            def __call__(self, ins):
                ins.then_inc(self.sem, 1)
                self.n += 1
                if self.before is None:
                    self.eng.wait_ge(self.sem, self.n)
                else:
                    self.eng.wait_ge(self.sem, self.before + (self.n - self.first))

            def enter(self, i, each):
                self.first, self.before, self.each = self.n, i * each + self.n, each

            def leave(self, times):
                assert self.n - self.first == self.each
                self.n, self.before = self.first + self.each * times, None

        def weights(pe, seg):
            pe.wait_ge(w_in_s[seg % 2], seg_ready[seg])
            return wring[seg % 2]

        block = ctx.enter_context(nc.Block())

        small_loads = [
            (c_sb[:, :], c_col), (b_sb[:, :], b_col), (qg[:, :], q_gain_col),
            (kg[:, :], k_gain.broadcast_to([P, A_LAT])), (gg[:, :], gdn_gain.broadcast_to([P, B_DIM])),
            (conv_sb[:, :, :], conv_col), (al[:, :], a_log.broadcast_to([P, B_HEADS])),
            (dtb[:, :], dt_bias.broadcast_to([P, B_HEADS])),
            (wuv[:, :, :], w_uv[0].rearrange("h r v -> r h v")),
        ]
        CONSTS = 16 * len(small_loads)
        x_tiles = x[0].rearrange("(t p) d -> p t d", p=P)

        conv_done = sem("conv_done")
        raw_done = sem("raw_done")
        l2_sq = sem("l2_sq")
        l2_mm = sem("l2_mm")
        l2_rt = sem("l2_rt")
        l2_done = sem("l2_done")
        gate_v = sem("gate_v")
        gate_s = sem("gate_s")
        gate_mm = sem("gate_mm")
        d_spread = sem("d_spread")
        d_pre = sem("d_pre")
        d_dif = sem("d_dif")
        d_exp = sem("d_exp")
        d_upper = sem("d_upper")
        d_tr = sem("d_tr")
        d_kv = sem("d_kv")
        d_us = sem("d_us")
        d_n1 = sem("d_n1")
        d_n1s = sem("d_n1s")
        d_dx = sem("d_dx")
        d_inv = sem("d_inv")
        d_ks = sem("d_ks")
        d_qs = sem("d_qs")
        d_res = sem("d_res")
        d_vn = sem("d_vn")
        d_vns = sem("d_vns")
        d_ds = sem("d_ds")
        d_state = sem("d_state")
        d_o = sem("d_o")
        d_osq = sem("d_osq")
        d_oms = sem("d_oms")
        d_ort = sem("d_ort")
        d_yb = sem("d_yb")
        d_yt = sem("d_yt")
        d_mix = sem("d_mix")
        H4 = B_HEADS
        LANES = [P, H4, P]

        def heads(ap):
            return ap.rearrange("p (h n) -> p h n", h=H4)

        def per_head(col):
            return col.unsqueeze(2).broadcast_to(LANES)

        def all_heads(tab):
            return tab.unsqueeze(1).broadcast_to(LANES)

        def hcol(h):
            return slice(h * P, (h + 1) * P)

        def chunk_of(j, c):
            return raw[:, j, CONV_W - 1 + c * P:CONV_W - 1 + (c + 1) * P]

        def gate(k, c=None):
            v = gates[:, k, :]
            return v if c is None else v[:, c * H4:(c + 1) * H4]

        (G_X, G_ABS, G_EXP, G_LN, G_POS, G_SP, G_G, G_BETA, G_CUM, G_ECUM, G_LAST, G_EDEC, G_ELAST, G_NBE,
         G_ALOG, G_DIF) = range(16)

        def delta_dve(dve, step):
            for j in range(12):
                if j >= 2:
                    dve.wait_ge(raw_done, j - 1)
                o = cv[j % 2]
                if j == 0:
                    dve.wait_ge(proj_out, N_QKV)
                step(dve.tensor_scalar(o, raw[:, j, 0:S], conv_sb[:, j, 0:1], None, ALU.mult))
                for w in range(1, CONV_W):
                    ins = dve.scalar_tensor_tensor(out=o, in0=raw[:, j, w:w + S], scalar=conv_sb[:, j, w:w + 1],
                                                   in1=o, op0=ALU.mult, op1=ALU.add)
                    if w < CONV_W - 1:
                        step(ins)
                    else:
                        ins.then_inc(conv_done, 1)
            t3 = [P, NT, H4]

            def g3(k):
                return gates[:, k, :].rearrange("p (t h) -> p t h", h=H4)
            step(dve.tensor_tensor(g3(G_X), small[:, :, 132:136], dtb[:, :].unsqueeze(1).broadcast_to(t3), ALU.add))
            step(dve.tensor_scalar(gate(G_POS), gate(G_X), 0.0, None, ALU.max))
            dve.scalar_tensor_tensor(out=gate(G_ABS), in0=gate(G_POS), scalar=2.0, in1=gate(G_X), op0=ALU.mult,
                                     op1=ALU.subtract).then_inc(gate_v, 1)
            dve.wait_ge(gate_s, 4)
            step(dve.tensor_tensor(gate(G_SP), gate(G_LN), gate(G_POS), ALU.add))
            step(dve.tensor_scalar(gate(G_SP), gate(G_SP), -1.0, None, ALU.mult))
            step(dve.tensor_tensor(g3(G_G), g3(G_SP), gates[:, G_ALOG, 0:H4].unsqueeze(1).broadcast_to(t3), ALU.mult))
            step(dve.tensor_scalar(gate(G_BETA), gate(G_BETA), 1.0, None, ALU.add))
            dve.reciprocal(gate(G_BETA), gate(G_BETA)).then_inc(gate_v, 1)
            dve.wait_ge(gate_s, 8)
            dve.tensor_tensor(gate(G_DIF), gate(G_LAST), gate(G_CUM), ALU.subtract).then_inc(gate_v, 1)
            dve.wait_ge(gate_v, 2)
            step(dve.tensor_tensor(gate(G_NBE), gate(G_BETA), gate(G_ECUM), ALU.mult))
            step(dve.tensor_scalar(gate(G_NBE), gate(G_NBE), -1.0, None, ALU.mult))
            for j in range(2 * H4):
                dve.wait_ge(l2_rt, j + 1)
                step(dve.reciprocal(norm[j % 2], norm[j % 2]))
                dve.tensor_tensor(raw[:, j, CONV_W - 1:], raw[:, j, CONV_W - 1:], norm[j % 2],
                                  ALU.mult).then_inc(l2_done, 1)
            step(dve.memset(state, 0.0))
            for c in range(NT):
                t0 = c * (LEVELS + 0)
                dve.wait_ge(d_pre, 4 * c + 1)
                if c == 0:
                    dve.wait_ge(gate_s, 9)
                    dve.wait_ge(l2_done, 2 * H4)
                for h in range(H4):
                    ins = dve.tensor_scalar(grow[:, hcol(h)], bank(0)[:, hcol(h)], gate(G_CUM, c)[:, h:h + 1], 0.0,
                                            ALU.subtract, ALU.min)
                    step(ins) if h < H4 - 1 else ins.then_inc(d_dif, 1)
                dve.wait_ge(d_exp, c + 1)
                step(dve.tensor_tensor(heads(decayT), heads(decayT), all_heads(triu[:, :]), ALU.mult))
                dve.wait_ge(d_pre, 4 * c + 4)
                step(dve.tensor_tensor(attnT, bank(3), decayT, ALU.mult))
                step(dve.tensor_tensor(upper, bank(2), decayT, ALU.mult))
                dve.tensor_tensor(upper, upper, bank(1), ALU.mult).then_inc(d_upper, 1)
                for x in range(2):
                    step(dve.tensor_copy(heads(inv[:, x, :]), all_heads(ident[:, :])))
                dve.wait_ge(d_tr, 2 * c + 2)
                step(dve.tensor_tensor(heads(kdec), heads(bank(4)), per_head(gate(G_EDEC, c)), ALU.mult))
                dve.tensor_tensor(heads(bv), heads(bank(5)), per_head(gate(G_BETA, c)), ALU.mult).then_inc(d_kv, 1)
                for l in range(LEVELS):
                    last = l == LEVELS - 1
                    dve.wait_ge(d_dx, c * LEVELS + l + 1)
                    if not last:
                        step(dve.tensor_tensor(inv[:, 0, :], inv[:, 0, :], bank(0), ALU.subtract))
                    dve.tensor_tensor(inv[:, 1, :], inv[:, 1, :], bank(7), ALU.subtract).then_inc(d_inv, 1)
                dve.wait_ge(d_ks, 2 * c + 2)
                dve.wait_ge(d_kv, c + 1)
                for h in range(H4):
                    ins = dve.scalar_tensor_tensor(out=resid[:, hcol(h)], in0=bank(1)[:, hcol(h)],
                                                   scalar=gate(G_NBE, c)[:, h:h + 1], in1=bv[:, hcol(h)],
                                                   op0=ALU.mult, op1=ALU.add)
                    step(ins) if h < H4 - 1 else ins.then_inc(d_res, 1)
                dve.wait_ge(d_ds, 2 * c + 2)
                for h in range(H4):
                    ins = dve.scalar_tensor_tensor(out=state[:, hcol(h)], in0=state[:, hcol(h)],
                                                   scalar=gate(G_ELAST, c)[:, h:h + 1], in1=bank(4)[:, hcol(h)],
                                                   op0=ALU.mult, op1=ALU.add)
                    step(ins) if h < H4 - 1 else ins.then_inc(d_state, 1)
                dve.wait_ge(d_qs, c + 1)
                dve.tensor_tensor(o_sb, qse, bank(5), ALU.add).then_inc(d_o, 1)
                step(dve.tensor_tensor(heads(z[:, c, :]), heads(z[:, c, :]), all_heads(gg[:, :]), ALU.mult))
                dve.wait_ge(d_osq, c * H4 + H4)
                dve.tensor_scalar(ost[:, 1, :], ost[:, 0, :], 1.0 / B_DIM, EPS, ALU.mult, ALU.add).then_inc(d_oms, 1)
                dve.wait_ge(d_ort, c + 1)
                step(dve.reciprocal(ost[:, 3, :], ost[:, 2, :]))
                for h in range(H4):
                    ins = dve.scalar_tensor_tensor(out=yb[:, hcol(h)], in0=o_sb[:, hcol(h)],
                                                   scalar=ost[:, 3, h:h + 1], in1=z[:, c, hcol(h)],
                                                   op0=ALU.mult, op1=ALU.mult)
                    step(ins) if h < H4 - 1 else ins.then_inc(d_yb, 1)

        def delta_act(act, link):
            for j in range(12):
                act.wait_ge(conv_done, j + 1)
                act.activation(raw[:, j, CONV_W - 1:], cv[j % 2], ACT.Silu).then_inc(raw_done, 1)
            act.wait_ge(gate_v, 1)
            act.activation(gate(G_EXP), gate(G_ABS), ACT.Exp, scale=-1.0).then_inc(gate_s, 1)
            act.activation(gates[:, G_ALOG, 0:H4], al[:, :], ACT.Exp).then_inc(gate_s, 1)
            act.activation(gates[:, G_BETA, :].rearrange("p (t h) -> p t h", h=H4), small[:, :, 136:140], ACT.Exp,
                           scale=-1.0).then_inc(gate_s, 1)
            act.wait_ge(gate_s, 1)
            act.activation(gate(G_LN), gate(G_EXP), ACT.Ln, bias=ones[:, 0:1]).then_inc(gate_s, 1)
            act.wait_ge(gate_mm, 1)
            act.activation(gate(G_CUM), bank(0)[:, 0:32], ACT.Copy).then_inc(gate_s, 1)
            act.activation(gate(G_LAST), bank(0)[:, 32:64], ACT.Copy).then_inc(gate_s, 1)
            act.activation(gate(G_ECUM), bank(0)[:, 0:32], ACT.Exp).then_inc(gate_s, 1)
            act.activation(gate(G_ELAST), bank(0)[:, 32:64], ACT.Exp).then_inc(gate_s, 1)
            act.wait_ge(gate_v, 3)
            act.activation(gate(G_EDEC), gate(G_DIF), ACT.Exp).then_inc(gate_s, 1)
            for j in range(2 * H4):
                if j >= 2:
                    act.wait_ge(l2_done, j - 1)
                else:
                    act.wait_ge(raw_done, 12)
                act.activation(norm[j % 2], raw[:, j, CONV_W - 1:], ACT.Square).then_inc(l2_sq, 1)
                act.wait_ge(l2_mm, j + 1)
                q = j < H4
                act.activation(norm[j % 2], pair[2 + j % 2][:, :], ACT.Sqrt, scale=float(B_DIM) if q else 1.0,
                               bias=eps[:, 1:2] if q else eps[:, 0:1]).then_inc(l2_rt, 1)
            for c in range(NT):
                act.wait_ge(d_dif, c + 1)
                act.activation(decayT, grow, ACT.Exp).then_inc(d_exp, 1)
                for l in range(LEVELS):
                    i = c * LEVELS + l
                    act.wait_ge(d_n1, i + 1)
                    act.activation(n1, bank(6), ACT.Copy).then_inc(d_n1s, 1)
                act.wait_ge(d_ks, 2 * c + 2)
                if c:
                    act.wait_ge(d_o, c)
                for h in range(H4):
                    ins = act.activation(qse[:, hcol(h)], bank(2)[:, hcol(h)], ACT.Copy,
                                         scale=gate(G_ECUM, c)[:, h:h + 1])
                    link(ins) if h < H4 - 1 else ins.then_inc(d_qs, 1)
                act.wait_ge(d_vn, c + 1)
                act.activation(vnew, bank(3), ACT.Copy).then_inc(d_vns, 1)
                act.wait_ge(d_o, c + 1)
                for h in range(H4):
                    act.wait_ge(d_osq, c * H4 + h) if c + h else None
                    act.activation(sqj[:, hcol(h)], o_sb[:, hcol(h)], ACT.Square,
                                   accum_out=ost[:, 0, h:h + 1]).then_inc(d_osq, 1)
                act.wait_ge(d_oms, c + 1)
                act.activation(ost[:, 2, :], ost[:, 1, :], ACT.Sqrt).then_inc(d_ort, 1)
                act.wait_ge(d_yt, c + 1)
                act.activation(mixT[:, H4:2 * H4, c * P:(c + 1) * P], heads(bank(6)), ACT.Copy).then_inc(d_mix, 1)

        def delta_pool(pool, step):
            pool.wait_ge(gate_v, 2)
            for c in range(NT):
                if c:
                    pool.wait_ge(d_pre, 4 * c)
                pool.tensor_copy(heads(spread[:, 0, :]), per_head(gate(G_G, c))).then_inc(d_spread, 1)
                pool.tensor_copy(heads(spread[:, 1, :]), per_head(gate(G_BETA, c))).then_inc(d_spread, 1)
                pool.wait_ge(d_upper, c + 1)
                for l in range(LEVELS):
                    i = c * LEVELS + l
                    if i >= 2:
                        pool.wait_ge(d_n1, i - 1)
                    pool.tensor_tensor(heads(upper_s[i % 2]), heads(upper), all_heads(level[:, l, :]),
                                       ALU.mult).then_inc(d_us, 1)

        def delta_pe(pe):
            pe.wait_ge(gate_v, 2)
            pe.wait_ge(proj_out, len(jobs))
            pe.matmul(bank(0)[:, 0:32], triu[:, :], gate(G_G), start=True, stop=True)
            pe.matmul(bank(0)[:, 32:64], ones[:, :], gate(G_G), start=True, stop=True).then_inc(gate_mm, 1)
            for j in range(2 * H4):
                pe.wait_ge(l2_sq, j + 1)
                if j >= 2:
                    pe.wait_ge(l2_rt, j - 1)
                for hf in range(2):
                    ins = pe.matmul(pair[2 + j % 2][:, hf * HALF:(hf + 1) * HALF], ones[:, :],
                                    norm[j % 2][:, hf * HALF:(hf + 1) * HALF], start=True, stop=True)
                ins.then_inc(l2_mm, 1)
            for c in range(NT):
                pe.wait_ge(d_spread, 2 * c + 2)
                if c == 0:
                    pe.wait_ge(gate_s, 9)
                    pe.wait_ge(l2_done, 2 * H4)
                else:
                    pe.wait_ge(d_state, c)
                    pe.wait_ge(d_qs, c)
                for h in range(H4):
                    ins = pe.matmul(bank(0)[:, hcol(h)], spread[:, 0, hcol(h)], triu[:, :], start=True, stop=True)
                ins.then_inc(d_pre, 1)
                for h in range(H4):
                    ins = pe.matmul(bank(1)[:, hcol(h)], spread[:, 1, hcol(h)], ident[:, :], start=True, stop=True)
                ins.then_inc(d_pre, 1)
                for h in range(H4):
                    ins = pe.matmul(bank(2)[:, hcol(h)], chunk_of(H4 + h, c), chunk_of(H4 + h, c), start=True,
                                    stop=True)
                ins.then_inc(d_pre, 1)
                for h in range(H4):
                    ins = pe.matmul(bank(3)[:, hcol(h)], chunk_of(H4 + h, c), chunk_of(h, c), start=True, stop=True)
                ins.then_inc(d_pre, 1)
                if c:
                    pe.wait_ge(d_o, c)
                for i, j0 in enumerate((H4, 2 * H4)):
                    for h in range(H4):
                        ins = pe.transpose(bank(4 + i)[:, hcol(h)], chunk_of(j0 + h, c), ident[:, :])
                    ins.then_inc(d_tr, 1)
                for l in range(LEVELS):
                    i = c * LEVELS + l
                    pe.wait_ge(d_us, i + 1)
                    if l:
                        pe.wait_ge(d_inv, i)
                    else:
                        pe.wait_ge(d_kv, c + 1)
                        if c:
                            pe.wait_ge(d_mix, c)
                    for h in range(H4):
                        ins = pe.matmul(bank(6)[:, hcol(h)], upper_s[i % 2][:, hcol(h)], inv[:, 0, hcol(h)],
                                        start=True, stop=True)
                    ins.then_inc(d_n1, 1)
                    pe.wait_ge(d_n1s, i + 1)
                    if l < LEVELS - 1:
                        for h in range(H4):
                            pe.matmul(bank(0)[:, hcol(h)], inv[:, 1, hcol(h)], n1[:, hcol(h)], start=True, stop=True)
                    for h in range(H4):
                        ins = pe.matmul(bank(7)[:, hcol(h)], n1[:, hcol(h)], inv[:, 1, hcol(h)], start=True,
                                        stop=True)
                    ins.then_inc(d_dx, 1)
                for i, j0 in enumerate((H4, 0)):
                    for h in range(H4):
                        ins = pe.matmul(bank(1 + i)[:, hcol(h)], chunk_of(j0 + h, c), state[:, hcol(h)], start=True,
                                        stop=True)
                    ins.then_inc(d_ks, 1)
                pe.wait_ge(d_res, c + 1)
                pe.wait_ge(d_inv, (c + 1) * LEVELS)
                for h in range(H4):
                    ins = pe.matmul(bank(3)[:, hcol(h)], inv[:, 1, hcol(h)], resid[:, hcol(h)], start=True, stop=True)
                ins.then_inc(d_vn, 1)
                pe.wait_ge(d_vns, c + 1)
                for h in range(H4):
                    ins = pe.matmul(bank(4)[:, hcol(h)], kdec[:, hcol(h)], vnew[:, hcol(h)], start=True, stop=True)
                ins.then_inc(d_ds, 1)
                for h in range(H4):
                    ins = pe.matmul(bank(5)[:, hcol(h)], attnT[:, hcol(h)], vnew[:, hcol(h)], start=True, stop=True)
                ins.then_inc(d_ds, 1)
                pe.wait_ge(d_yb, c + 1)
                for h in range(H4):
                    ins = pe.transpose(bank(6)[:, hcol(h)], yb[:, hcol(h)], ident[:, :])
                ins.then_inc(d_yt, 1)

        a_ksq = sem("a_ksq")
        a_kms = sem("a_kms")
        a_krt = sem("a_krt")
        a_k = sem("a_k")
        a_ktr = sem("a_ktr")
        a_kT = sem("a_kT")
        a_in = [sem(f"a_in{i}") for i in range(2)]
        a_qsq = sem("a_qsq")
        a_qms = sem("a_qms")
        a_qrt = sem("a_qrt")
        a_qn = sem("a_qn")
        a_qtr = sem("a_qtr")
        a_qT = sem("a_qT")
        a_dm = sem("a_dm")
        a_bias = sem("a_bias")
        a_s = sem("a_s")
        a_sm = sem("a_sm")
        a_max = sem("a_max")
        a_p = sem("a_p")
        a_pt = sem("a_pt")
        a_pta = sem("a_pta")
        a_ptv = sem("a_ptv")
        a_o = sem("a_o")
        a_oT = sem("a_oT")
        a_ya = sem("a_ya")
        a_yas = sem("a_yas")
        a_rs = sem("a_rs")
        a_yt = sem("a_yt")
        a_mix = sem("a_mix")
        NK = [qb + 1 for qb in range(NT)]
        GA = [A_HEADS * qb for qb in range(NT + 1)]
        GV = [A_HEADS * sum(1 for x in range(qb) if NK[x] > 4) for qb in range(NT + 1)]

        def attention_sp(sp):
            for i in range(2):
                sp.wait_ge(aq_out[i], 16 * NT)
            for qb in range(NT):
                if qb == 0:
                    sp.wait_ge(d_mix, NT)
                if qb >= 2:
                    sp.wait_ge(a_qtr, 2 * (qb - 1))
                sp.dma_start(aqt[qb % 2], aq_dram[qb * P:(qb + 1) * P, :].rearrange("p (h n) -> p h n", h=A_HEADS)
                             ).then_inc(a_in[qb % 2], 16)

        def attention_pool(pool, step):
            pool.wait_ge(topk_done, len(QBS) + 1)
            pool.wait_ge(d_mix, NT)
            for qb in range(NT):
                n = P * NK[qb]
                if qb:
                    pool.wait_ge(a_bias, A_HEADS * qb)
                pool.tensor_tensor(dm[:, 0:n], mask[:, MOFF[qb]:MOFF[qb + 1]], dist[:, S - n:S],
                                   ALU.add).then_inc(a_dm, 1)
                pool.wait_ge(a_dm, qb + 1)
                for h in range(A_HEADS):
                    i = A_HEADS * qb + h
                    if i >= 2:
                        pool.wait_ge(a_sm, i - 1)
                    pool.tensor_scalar(bias[i % 2][:, 0:n], dm[:, 0:n], SLOPES[h], None,
                                       ALU.mult).then_inc(a_bias, 1)

        def attention_act(act, link):
            for t in range(NT):
                if t:
                    act.wait_ge(a_ksq, t)
                act.activation(sq_junk, small[:, t, 0:A_LAT], ACT.Square, accum_out=kst[:, 0, t:t + 1]
                               ).then_inc(a_ksq, 1)
            act.wait_ge(a_kms, 1)
            act.activation(kst[:, 2, :], kst[:, 1, :], ACT.Sqrt).then_inc(a_krt, 1)
            for i in range(2):
                act.wait_ge(a_ktr, i + 1)
                act.activation(kT[:, i * HALF:(i + 1) * HALF], bank(i), ACT.Copy).then_inc(a_kT, 1)
            for qb in range(NT):
                n = P * NK[qb]
                act.wait_ge(a_in[qb % 2], 16 * (qb // 2 + 1))
                if qb:
                    act.wait_ge(a_qrt, qb)
                for h in range(A_HEADS):
                    act.wait_ge(a_qsq, A_HEADS * qb + h) if qb + h else act.wait_ge(a_ksq, NT)
                    act.activation(sq_junk, aqt[qb % 2][:, h, :], ACT.Square, accum_out=qst[:, 0, h:h + 1]
                                   ).then_inc(a_qsq, 1)
                act.wait_ge(a_qms, qb + 1)
                act.activation(qst[:, 2, :], qst[:, 1, :], ACT.Sqrt).then_inc(a_qrt, 1)
                for i in range(2):
                    act.wait_ge(a_qtr, 2 * qb + i + 1)
                    if qb:
                        act.wait_ge(a_s, A_HEADS * qb)
                    act.activation(qT[:, 4 * i:4 * i + 4, :], bank(i).rearrange("p (h n) -> p h n", h=4), ACT.Copy,
                                   scale=qg[:, 0:1]).then_inc(a_qT, 1)

                def take_out(h):
                    i = A_HEADS * qb + h
                    act.wait_ge(a_pt, GA[qb] + GV[qb] + (2 if NK[qb] > 4 else 1) * h + 1)
                    if i >= 4:
                        act.wait_ge(a_o, i // 4)
                    w = min(4, NK[qb])
                    act.activation(PT[:, 0:w, h % 4, :], bank(6)[:, 0:w * P].rearrange("p (k n) -> p k n", k=w),
                                   ACT.Copy).then_inc(a_pta, 1)

                def o_out(g):
                    act.wait_ge(a_o, 2 * qb + g + 1)
                    act.activation(oT[:, 4 * g:4 * g + 4, :], bank(g).rearrange("p (h n) -> p h n", h=4),
                                   ACT.Copy).then_inc(a_oT, 1)

                for h in range(A_HEADS):
                    i = A_HEADS * qb + h
                    act.wait_ge(a_max, i + 1)
                    if i >= 2:
                        act.wait_ge(a_pt, GA[qb] + GV[qb] + (2 if NK[qb] > 4 else 1) * (h - 1) if h > 1 else
                                    (GA[qb] + GV[qb] - (2 if NK[qb - 1] > 4 else 1) * (1 - h)))
                    if qb and h == 0:
                        act.wait_ge(a_rs, qb)
                    act.activation(pr[i % 2][:, 0:n], sc[i % 2][:, 0:n], ACT.Exp, bias=smax[:, 1, h:h + 1],
                                   accum_out=smax[:, 2, h:h + 1]).then_inc(a_p, 1)
                    if h >= 1:
                        take_out(h - 1)
                    if h == 5:
                        o_out(0)
                take_out(A_HEADS - 1)
                o_out(1)
                act.wait_ge(a_yt, qb + 1)
                act.activation(mixT[:, 0:4, qb * P:(qb + 1) * P], heads(bank(1)), ACT.Copy).then_inc(a_mix, 1)

        def attention_dve(dve, step):
            step(dve.tensor_scalar(qg[:, :], qg[:, :], ATT_SCALE, None, ALU.mult))
            dve.wait_ge(a_ksq, NT)
            dve.tensor_scalar(kst[:, 1, :], kst[:, 0, :], 1.0 / A_LAT, EPS, ALU.mult, ALU.add).then_inc(a_kms, 1)
            dve.wait_ge(a_krt, 1)
            step(dve.reciprocal(kst[:, 3, :], kst[:, 2, :]))
            for t in range(NT):
                dve.scalar_tensor_tensor(out=ktok[:, t, :], in0=small[:, t, 0:A_LAT], scalar=kst[:, 3, t:t + 1],
                                         in1=kg[:, :], op0=ALU.mult, op1=ALU.mult).then_inc(a_k, 1)
            for qb in range(NT):
                n = P * NK[qb]
                dve.wait_ge(a_qsq, A_HEADS * (qb + 1))
                dve.tensor_scalar(qst[:, 1, :], qst[:, 0, :], 1.0 / A_LAT, EPS, ALU.mult, ALU.add).then_inc(a_qms, 1)
                dve.wait_ge(a_qrt, qb + 1)
                step(dve.reciprocal(qst[:, 3, :], qst[:, 2, :]))
                dve.tensor_tensor(aqt[qb % 2], aqt[qb % 2],
                                  qst[:, 3, :].unsqueeze(2).broadcast_to([P, A_HEADS, A_LAT]), ALU.mult
                                  ).then_inc(a_qn, 1)
                for h in range(A_HEADS):
                    i = A_HEADS * qb + h
                    dve.wait_ge(a_s, i + 1)
                    dve.wait_ge(a_bias, i + 1)
                    if i >= 2:
                        dve.wait_ge(a_p, i - 1)
                    dve.tensor_tensor_reduce(out=sc[i % 2][:, 0:n], in0=bias[i % 2][:, 0:n],
                                             in1=pair[1 + i % 2][:, 0:n], scale=1.0, scalar=TAKEN, op0=ALU.add,
                                             op1=ALU.max, accum_out=smax[:, 0, h:h + 1]).then_inc(a_sm, 1)
                    dve.wait_ge(a_sm, i + 1)
                    dve.tensor_scalar(smax[:, 1, h:h + 1], smax[:, 0, h:h + 1], -1.0, None,
                                      ALU.mult).then_inc(a_max, 1)
                    if NK[qb] > 4 and h:
                        rest_out(dve, qb, h - 1)
                if NK[qb] > 4:
                    rest_out(dve, qb, A_HEADS - 1)
                dve.wait_ge(a_p, A_HEADS * (qb + 1))
                dve.reciprocal(smax[:, 2, :], smax[:, 2, :]).then_inc(a_rs, 1)
                dve.wait_ge(a_rs, qb + 1)
                dve.wait_ge(a_ya, qb + 1)
                dve.tensor_tensor(ya.rearrange("p (h n) -> p h n", h=A_HEADS),
                                  bank(0).rearrange("p (h n) -> p h n", h=A_HEADS),
                                  smax[:, 2, :].unsqueeze(2).broadcast_to([P, A_HEADS, A_VDIM]), ALU.mult
                                  ).then_inc(a_yas, 1)

        def rest_out(dve, qb, h):
            i = A_HEADS * qb + h
            dve.wait_ge(a_pt, GA[qb] + GV[qb] + 2 * h + 2)
            dve.wait_ge(a_o, i // 4)
            w = NK[qb] - 4
            dve.tensor_copy(PT[:, 4:4 + w, h % 4, :], bank(7)[:, 0:w * P].rearrange("p (k n) -> p k n", k=w)
                            ).then_inc(a_ptv, 1)

        def attention_pe(pe):
            pe.wait_ge(a_k, NT)
            pe.wait_ge(d_mix, NT)
            for i in range(2):
                for q in range(4):
                    ins = pe.transpose(bank(i)[:, q * P:(q + 1) * P], ktok[:, 4 * i + q, :], ident[:, :])
                ins.then_inc(a_ktr, 1)
            for qb in range(NT):
                n = P * NK[qb]
                pe.wait_ge(a_qn, qb + 1)
                if qb:
                    pe.wait_ge(a_mix, qb)
                else:
                    pe.wait_ge(a_kT, 2)
                for i in range(2):
                    for q in range(4):
                        ins = pe.transpose(bank(i)[:, q * P:(q + 1) * P], aqt[qb % 2][:, 4 * i + q, :], ident[:, :])
                    ins.then_inc(a_qtr, 1)

                def scores(h):
                    i = A_HEADS * qb + h
                    pe.wait_ge(a_qT, 2 * qb + h // 4 + 1)
                    if i >= 2:
                        pe.wait_ge(a_sm, i - 1)
                    for c0 in range(0, n, HALF):
                        w = min(HALF, n - c0)
                        ins = pe.matmul(pair[1 + i % 2][:, c0:c0 + w], qT[:, h, :], kT[:, c0:c0 + w], start=True,
                                        stop=True)
                    ins.then_inc(a_s, 1)

                def turn(h):
                    i = A_HEADS * qb + h
                    pe.wait_ge(a_p, i + 1)
                    for g0 in range(0, NK[qb], 4):
                        w = min(4, NK[qb] - g0)
                        if g0:
                            if GV[qb] + h:
                                pe.wait_ge(a_ptv, GV[qb] + h)
                        elif i:
                            pe.wait_ge(a_pta, i)
                        for q in range(w):
                            ins = pe.transpose(bank(6 + g0 // 4)[:, q * P:(q + 1) * P],
                                               pr[i % 2][:, (g0 + q) * P:(g0 + q + 1) * P], ident[:, :])
                        ins.then_inc(a_pt, 1)

                def values(g):
                    pe.wait_ge(a_pta, GA[qb] + 4 * g + 4)
                    if NK[qb] > 4:
                        pe.wait_ge(a_ptv, GV[qb] + 4 * g + 4)
                    for k in range(NK[qb]):
                        ins = pe.matmul(bank(g), ktok[:, k, :], PT[:, k, :, :], start=(k == 0),
                                        stop=(k == NK[qb] - 1))
                    ins.then_inc(a_o, 1)

                scores(0)
                for h in range(A_HEADS):
                    if h + 1 < A_HEADS:
                        scores(h + 1)
                    turn(h)
                    if h == 3:
                        values(0)
                values(1)
                pe.wait_ge(a_oT, 2 * qb + 2)
                for h in range(A_HEADS):
                    ins = pe.matmul(bank(0)[:, h * A_VDIM:(h + 1) * A_VDIM], oT[:, h, :], wuv[:, h, :], start=True,
                                    stop=True)
                ins.then_inc(a_ya, 1)
                pe.wait_ge(a_yas, qb + 1)
                for q in range(4):
                    ins = pe.transpose(bank(1)[:, q * P:(q + 1) * P], ya[:, q * P:(q + 1) * P], ident[:, :])
                ins.then_inc(a_yt, 1)

        bg_in = sem("bg_in")
        gate_row = sem("gate_row")
        x1_mul = sem("x1_mul")
        x1_done = sem("x1_done")
        x1_out = [sem(f"x1_out{i}") for i in range(2)]
        x1_spill = x1_dram.rearrange("(t p) d -> p t d", p=P)

        def residual_sp(sp):
            sp.wait_ge(a_mix, NT)
            sp.dma_start(xbuf[:, :, :], x_tiles).then_inc(x2_in, 16)
            sp.dma_start(sub[:, :, :], subT).then_inc(sub_in, 16)
            sp.dma_start(bg[:, :, :], b_gate.unsqueeze(0).broadcast_to([P, 2, D])).then_inc(bg_in, 16)

        def spill_sp(sp):
            for hf in range(2):
                sp.wait_ge(x1_done, 12 + 4 * hf)
                sp.dma_start(x1_spill[:, 4 * hf:4 * hf + 4, :], xbuf[:, 4 * hf:4 * hf + 4, :]
                             ).then_inc(x1_out[hf], 16)

        def gate_row_pe(pe, name, n0):
            for i in range(2):
                w = weights(pe, seg0[name] + i)
                for kc in range(KC):
                    ins = pe.matmul(bank(4 + i), c_rep[:, kc, :], w[:, kc, :], start=(kc == 0), stop=(kc == KC - 1))
                ins.then_inc(ada_mm, 1)

        def gate_row_dve(dve, which, row, n0):
            for i in range(2):
                dve.wait_ge(ada_mm, n0 + i + 1)
                dve.tensor_tensor(row[:, i * HALF:(i + 1) * HALF], bank(4 + i), bg[:, which, i * HALF:(i + 1) * HALF],
                                  ALU.add).then_inc(gate_row, 1)

        def residual_pe(pe):
            pe.wait_ge(a_mix, NT)
            gate_row_pe(pe, "gate1", 4)
            for hf in range(2):
                w = weights(pe, seg0["out"] + hf)
                for t in range(NT):
                    n = hf * NT + t
                    if n >= 4:
                        pe.wait_ge(x1_mul, n - 3)
                    for kc in range(KC):
                        ins = pe.matmul(bank(n % 4), mixT[:, kc, t * P:(t + 1) * P], w[:, kc, :], start=(kc == 0),
                                        stop=(kc == KC - 1))
                    ins.then_inc(out_mm, 1)
            pe.wait_ge(gate_row, 2)
            ada_cols_pe(pe, 2, "scale2", 6)
            ada_cols_pe(pe, 3, "shift2", 8)
            xnorm_pe(pe, 1)

        def residual_dve(dve, step):
            dve.wait_ge(a_mix, NT)
            dve.wait_ge(bg_in, 16)
            gate_row_dve(dve, 0, grow1, 4)
            dve.wait_ge(gate_row, 2)
            dve.wait_ge(x2_in, 16)
            for hf in range(2):
                c0 = hf * HALF
                for t in range(NT):
                    n = hf * NT + t
                    dve.wait_ge(out_mm, n + 1)
                    if n >= 2:
                        dve.wait_ge(x1_done, n - 1)
                    dve.tensor_tensor(gmix[n % 2], bank(n % 4), grow1[:, c0:c0 + HALF], ALU.mult).then_inc(x1_mul, 1)
                    dve.wait_ge(x1_mul, n + 1)
                    dve.tensor_tensor(xbuf[:, t, c0:c0 + HALF], xbuf[:, t, c0:c0 + HALF], gmix[n % 2],
                                      ALU.add).then_inc(x1_done, 1)
            ada_cols_dve(dve, 2, 4, 6)
            ada_cols_dve(dve, 3, 3, 8)
            xnorm_dve(dve, 1, step)

        sub_in = sem("sub_in")
        q_out = sem("q_out")
        s_mm = sem("s_mm")
        s_out = sem("s_out")
        s_top = sem("s_top")
        c_max = sem("c_max")
        c_exp = sem("c_exp")
        c_sel = sem("c_sel")
        c_tr = sem("c_tr")
        c_T = sem("c_T")

        def search_pe(pe):
            for g in range(4):
                w = weights(pe, seg0["query"] + g)
                for n8 in range(8):
                    n = 8 * g + n8
                    if n == 0:
                        pe.wait_ge(hx_act, 16)
                        pe.wait_ge(hx_dve, 16)
                    if n >= 4:
                        pe.wait_ge(q_out, n - 3)
                    j, hf = n8 // 2, n8 % 2
                    for kc in range(KC):
                        ins = pe.matmul(bank(n % 4), w[:, kc, j * P:(j + 1) * P], h2T[:, kc, hf * HALF:(hf + 1) * HALF],
                                        start=(kc == 0), stop=(kc == KC - 1))
                    ins.then_inc(q_mm, 1)
                pe.wait_ge(q_out, 8 * g + 8)
                pe.wait_ge(sub_in, 16)
                for t in range(NT):
                    n = NT * g + t
                    if n >= 2:
                        pe.wait_ge(s_out, n - 1)
                    else:
                        pe.wait_ge(mods_done, 4)
                    for j in range(4):
                        ins = pe.matmul(bank(6 + n % 2)[:, j * NKEYS:(j + 1) * NKEYS], pqT[0][:, j, t * P:(t + 1) * P],
                                        sub[:, 4 * g + j, :], start=True, stop=True)
                    ins.then_inc(s_mm, 1)
            gate_row_pe(pe, "gate2", 10)
            for t in range(NT):
                pe.wait_ge(c_sel, t + 1)
                if t >= 2:
                    pe.wait_ge(c_T, t - 1)
                for i in range(3):
                    ins = pe.transpose(bank(t % 2)[:, i * P:(i + 1) * P], sel[t % 2][:, i, :], ident[:, :])
                ins.then_inc(c_tr, 1)

        def search_act(act, link):
            for g in range(4):
                for n8 in range(8):
                    n = 8 * g + n8
                    act.wait_ge(q_mm, n + 1)
                    if g:
                        act.wait_ge(s_mm, NT * g)
                    j, hf = n8 // 2, n8 % 2
                    act.activation(pqT[0][:, j, hf * HALF:(hf + 1) * HALF], bank(n % 4), ACT.Copy).then_inc(q_out, 1)
                for t in range(NT):
                    n = NT * g + t
                    act.wait_ge(s_mm, n + 1)
                    if n >= 2:
                        act.wait_ge(s_top, n - 1)
                    act.activation(s_st[n % 2], bank(6 + n % 2), ACT.Copy).then_inc(s_out, 1)
            for t in range(NT):
                act.wait_ge(c_max, t + 1)
                act.activation(ce, ce, ACT.Exp).then_inc(c_exp, 1)
                act.wait_ge(c_tr, t + 1)
                act.activation(selT[:, :, t * P:(t + 1) * P], bank(t % 2)[:, 0:3 * P].rearrange("p (a n) -> p a n", a=3),
                               ACT.Copy).then_inc(c_T, 1)

        def search_dve(dve, step):
            for g in range(4):
                for t in range(NT):
                    n = NT * g + t
                    dve.wait_ge(s_out, n + 1)
                    s_ = s_st[n % 2]
                    for j in range(4):
                        hp = 4 * g + j
                        row = s_[:, j * NKEYS:(j + 1) * NKEYS]
                        lo, hi = sh[:, t, hp, 0:8], sh[:, t, hp, 8:16]
                        ix = m_ix[:, j * PEER_TOPK:(j + 1) * PEER_TOPK]
                        step(dve.max(lo, row))
                        step(dve.max_index(ix[:, 0:8], lo, row))
                        step(dve.match_replace(out=s_tmp, in_to_replace=lo, in_values=row, imm_value=TAKEN))
                        step(dve.max(hi, s_tmp))
                        step(dve.max_index(ix[:, 8:16], hi, s_tmp))
                    dve.tensor_copy(ih[:, t, 4 * g:4 * g + 4, :], m_ix.rearrange("p (a k) -> p a k", a=4)
                                    ).then_inc(s_top, 1)
                    dve.wait_ge(s_top, n + 1)
            gate_row_dve(dve, 1, grow2, 10)
            K4 = [P, PEER_HEADS, PEER_TOPK, PEER_TOPK]
            K3 = [P, PEER_HEADS, PEER_TOPK]

            def by_head(v):
                return v.rearrange("p (h k) -> p h k", h=PEER_HEADS)

            def pick(dst, at, ids):
                step(dve.tensor_tensor(eq, by_head(at).unsqueeze(3).broadcast_to(K4),
                                       iota_c[:, 0:PEER_TOPK].unsqueeze(1).unsqueeze(1).broadcast_to(K4),
                                       ALU.is_equal))
                step(dve.tensor_tensor(eq, eq, ids.unsqueeze(2).broadcast_to(K4), ALU.mult))
                step(dve.tensor_reduce(by_head(dst), eq, AX.X, ALU.add))

            for t in range(NT):
                tab = sh[:, t, :, :].rearrange("p (h x) k -> p h x k", x=2)
                itab = ih[:, t, :, :].rearrange("p (h x) k -> p h x k", x=2)
                step(dve.tensor_tensor(cand.rearrange("p h (a b) -> p h a b", a=PEER_TOPK),
                                       tab[:, :, 0, :].unsqueeze(3).broadcast_to(K4),
                                       tab[:, :, 1, :].unsqueeze(2).broadcast_to(K4), ALU.add))
                for h in range(PEER_HEADS):
                    row = cand[:, h, :]
                    lo, hi = cs[:, h, 0:8], cs[:, h, 8:16]
                    ix = ci[:, h * PEER_TOPK:(h + 1) * PEER_TOPK]
                    step(dve.max(lo, row))
                    step(dve.max_index(ix[:, 0:8], lo, row))
                    step(dve.match_replace(out=cand2, in_to_replace=lo, in_values=row, imm_value=TAKEN))
                    step(dve.max(hi, cand2))
                    step(dve.max_index(ix[:, 8:16], hi, cand2))
                step(dve.tensor_tensor(ce, cs, cs[:, :, 0:1].broadcast_to(K3), ALU.subtract))
                step(dve.tensor_scalar(cab[:, 0, :], ci, 4, None, ALU.logical_shift_right))
                step(dve.tensor_scalar(cab[:, 1, :], ci, PEER_TOPK - 1, None, ALU.bitwise_and))
                dve.tensor_copy(cabf[:, :, :], cab[:, :, :]).then_inc(c_max, 1)
                dve.wait_ge(c_max, t + 1)
                if t >= 2:
                    dve.wait_ge(c_tr, t - 1)
                for x in range(2):
                    pick(sel[t % 2][:, x, :], cabf[:, x, :], itab[:, :, x, :])
                dve.wait_ge(c_exp, t + 1)
                step(dve.tensor_reduce(gs, ce, AX.X, ALU.add))
                step(dve.reciprocal(gs, gs))
                dve.tensor_tensor(by_head(sel[t % 2][:, 2, :]), ce, gs.unsqueeze(2).broadcast_to(K3), ALU.mult
                                  ).then_inc(c_sel, 1)
                dve.wait_ge(c_sel, t + 1)

        oh_ready = sem("oh_ready")
        g_mm = sem("g_mm")
        g_ev = sem("g_ev")
        g_out = [sem(f"g_out{i}") for i in range(2)]
        PER = G_TOK // 4

        def gates_dve(dve, step):
            dve.wait_ge(c_T, NT)
            with dve.Fori(0, S // 8) as i:
                for b in range(2):
                    dve.wait_ge(g_mm, i * 2 + (b + 1))
                    for q in range(4):
                        j = 4 * b + q
                        i1 = selT[:, 0, bass.ds(i * 8 + j, 1)]
                        i2 = selT[:, 1, bass.ds(i * 8 + j, 1)]
                        gt = selT[:, 2, bass.ds(i * 8 + j, 1)]
                        dve.tensor_scalar(oh1[:, j, :], iota_c[:, :], i1, None, ALU.is_equal)
                        ins = dve.tensor_scalar(oh2[:, j, :], iota_c[:, :], i2, gt, ALU.is_equal, ALU.mult)
                    ins.then_inc(oh_ready, 1)

        def gates_pe(pe):
            pe.wait_ge(gate_row, 4)
            pe.wait_ge(c_T, NT)
            pe.sem_inc(g_mm, 2)
            with pe.Fori(0, S // 8) as i:
                for b in range(2):
                    pe.wait_ge(oh_ready, i * 2 + (b + 1))
                    pe.wait_ge(g_ev, i * 2 + (b + 1))
                    for q in range(4):
                        j = 4 * b + q
                        ins = pe.matmul(bank(2 * b)[:, q * P:(q + 1) * P], oh1[:, j, :], oh2[:, j, :], start=True,
                                        stop=True)
                    ins.then_inc(g_mm, 1)

        def gates_act(act, link):
            act.sem_inc(g_ev, 2)

            def block_out(m, x):
                with act.Fori(0, PER // 2) as k:
                    for b in range(2):
                        act.wait_ge(g_mm, m * (2 * PER) + k * 2 + (PER * x + b + 3))
                        act.activation(gst[x][:, :, bass.ds(k * 8 + 4 * b, 4)],
                                       bank(2 * b).rearrange("p (t i) -> p i t", t=4), ACT.Copy
                                       ).then_inc(g_ev, 1)

            for x in range(2):
                block_out(0, x)
            with act.Fori(1, G_BLOCKS // 2) as m:
                for x in range(2):
                    act.wait_ge(g_out[x], m * 16)
                    block_out(m, x)

        def gates_sp(sp):
            with sp.Fori(0, G_BLOCKS // 2) as m:
                for x in range(2):
                    sp.wait_ge(g_ev, m * (2 * PER) + (PER * (x + 1) + 2))
                    sp.dma_start(g_dram[bass.ds(m * 2 + x, 1), :, :, :].rearrange("b p i t -> p (b i) t"),
                                 gst[x]).then_inc(g_out[x], 16)
            for x in range(2):
                sp.wait_ge(g_out[x], 8 * G_BLOCKS)

        u_in = [sem(f"u_in{j}") for j in range(SG)]
        v_in = [sem(f"v_in{i}") for i in range(2)]
        gg_in = [sem(f"gg_in{i}") for i in range(2)]
        e_mm = sem("e_mm")
        e_act = sem("e_act")
        e_mul = sem("e_mul")
        y_mm = sem("y_mm")
        y_add = sem("y_add")
        y_zero = sem("y_zero")
        y_fin = sem("y_fin")
        x3_in = sem("x3_in")
        out_out = [sem(f"out_out{i}") for i in range(2)]
        v_rows = v_tab

        def experts_sp(sp):
            def loads(s, x, first=False):
                for j in range(SG):
                    if not first:
                        sp.wait_ge(e_mm, s * SG + (j + 1 - SG))
                    sp.dma_start(u_sb[j], uT[bass.ds(s * SG + j, 1), :, :, :].rearrange("o p k n -> p (o k) n")
                                 ).then_inc(u_in[j], 16)
                if not (first or (isinstance(s, int) and s < 2)):
                    sp.wait_ge(e_mul, s * SG + (-SG))
                sp.dma_start(g_sb[x], g_dram.rearrange("b p i t -> p b i t")[:, :, bass.ds(s * SG, SG), :]
                             ).then_inc(gg_in[x], 16)
                if not (first or (isinstance(s, int) and s < 2)):
                    sp.wait_ge(y_mm, s * 16 + (-16))
                sp.dma_start(v_sb[x], v_rows[:, bass.ds(s * SG, SG), :]).then_inc(v_in[x], 16)
            loads(0, 0, True)
            loads(1, 1)
            with sp.Fori(1, NSG // 2) as m:
                for x in range(2):
                    loads(m * 2 + x, x)
            sp.wait_ge(y_mm, 16 * NSG)
            sp.dma_start(x1_in_sb[:, :, :], x1_spill).then_inc(x3_in, 16)
            out_tiles = out.rearrange("(t p) d -> p t d", p=P)
            for hf in range(2):
                sp.wait_ge(y_fin, 4 * (hf + 1))
                sp.dma_start(out_tiles[:, 4 * hf:4 * hf + 4, :], yacc[:, 4 * hf:4 * hf + 4, :]).then_inc(out_out[hf], 16)
            for hf in range(2):
                sp.wait_ge(out_out[hf], 16)

        def experts_pe(pe):
            def up(s, x, j, u_n):
                pe.wait_ge(u_in[j], u_n)
                if not (isinstance(s, int) and s * SG + j < 2):
                    pe.wait_ge(e_act, s * SG + (j - 1))
                for hf in range(2):
                    for kc in range(KC):
                        ins = pe.matmul(pair[j % 2][:, hf * HALF:(hf + 1) * HALF], u_sb[j][:, kc, :],
                                        h2T[:, kc, hf * HALF:(hf + 1) * HALF], start=(kc == 0), stop=(kc == KC - 1))
                ins.then_inc(e_mm, 1)

            def down(s, x, q):
                t, hf = q // 2, q % 2
                pe.wait_ge(y_add, s * 16 + (q + 1))
                for k in range(SG):
                    ins = pe.matmul(bank(4 + q % 4), actT[x][:, k, t * P:(t + 1) * P],
                                    v_sb[x][:, k, hf * HALF:(hf + 1) * HALF], start=(k == 0), stop=(k == SG - 1))
                ins.then_inc(y_mm, 1)

            def both(s, x, n_u, n_v):
                for j in range(SG):
                    up(s, x, j, n_u)
                    if j == 0:
                        pe.wait_ge(v_in[1 - x], n_v)
                        pe.wait_ge(e_mul, s * SG)
                    for q in range(4 * j, 4 * j + 4):
                        down(s + (-1), 1 - x, q)

            pe.wait_ge(g_ev, 2 * (S // 8) + 2)
            for j in range(SG):
                up(0, 0, j, 16)
            with pe.Fori(0, NSG // 2 - 1) as m:
                both(m * 2 + 1, 1, (m * 2 + 2) * 16, m * 16 + 16)
                both(m * 2 + 2, 0, (m * 2 + 3) * 16, m * 16 + 16)
            both(NSG - 1, 1, 16 * NSG, 8 * NSG)
            pe.wait_ge(v_in[1], 8 * NSG)
            pe.wait_ge(e_mul, SG * NSG)
            for q in range(16):
                down(NSG - 1, 1, q)

        def experts_act(act, link):
            def gelus(s, x, first):
                for j in range(SG):
                    act.wait_ge(e_mm, s * SG + (j + 1))
                    if j == 0 and not first:
                        act.wait_ge(y_mm, s * 16 + (-16))
                    act.activation(actT[x][:, j, :], pair[j % 2][:, :], ACT.Gelu).then_inc(e_act, 1)

            for x in range(2):
                gelus(x, x, True)
            with act.Fori(1, NSG // 2) as m:
                for x in range(2):
                    gelus(m * 2 + x, x, False)

        def experts_pool(pool, step):
            with pool.Fori(0, NSG // 2) as m:
                for x in range(2):
                    pool.wait_ge(gg_in[x], m * 16 + 16)
                    for j in range(SG):
                        pool.wait_ge(e_act, m * (2 * SG) + (x * SG + j + 1))
                        a_ = actT[x][:, j, :].rearrange("p (b t) -> p b t", t=G_TOK)
                        pool.tensor_tensor(a_, a_, g_sb[x][:, :, j, :], ALU.mult).then_inc(e_mul, 1)

        def experts_dve(dve, step):
            dve.wait_ge(hx_mm, 32)
            dve.memset(yacc[:, :, :], 0.0).then_inc(y_zero, 1)
            dve.wait_ge(y_zero, 1)
            dve.sem_inc(y_add, 4)
            with dve.Fori(0, NSG) as s:
                for q in range(16):
                    t, hf = q // 2, q % 2
                    dve.wait_ge(y_mm, s * 16 + (q + 1))
                    y_ = yacc[:, t, hf * HALF:(hf + 1) * HALF]
                    dve.tensor_tensor(y_, y_, bank(4 + q % 4), ALU.add).then_inc(y_add, 1)
            dve.wait_ge(x3_in, 16)
            dve.wait_ge(y_add, 16 * NSG + 4)
            for t in range(NT):
                step(dve.tensor_tensor(yacc[:, t, :], yacc[:, t, :], grow2, ALU.mult))
                dve.tensor_tensor(yacc[:, t, :], yacc[:, t, :], x1_in_sb[:, t, :], ALU.add).then_inc(y_fin, 1)

        @block.sync
        def _(sp):
            for dst, src in small_loads:
                sp.dma_start(dst, src).then_inc(consts_in, 16)
            def load_weights(first, end):
                for n in range(first, end):
                    if n >= 2:
                        sp.wait_ge(*released[n - 2])
                    for at, src in segs[n]:
                        w = src.shape[2]
                        sp.dma_start(wring[n % 2][:, :, at:at + w], src).then_inc(w_in_s[n % 2], 16)
            load_weights(0, seg0["out"])
            attention_sp(sp)
            residual_sp(sp)
            load_weights(seg0["out"], seg0["shift2"])
            spill_sp(sp)
            load_weights(seg0["shift2"], NSEG)
            gates_sp(sp)
            experts_sp(sp)

        @block.gpsimd
        def _(pool):
            step = Steps(pool, pool_const)
            for t_, v in ((ident, 0.0), (ones, 1.0), (triu, 1.0), (causal, 0.0)):
                pool.memset(t_[:, :], v).then_inc(pool_const, 1)
            pool.memset(level[:, :, :], 0.0).then_inc(pool_const, 1)
            pool.memset(eps[:, 0:1], EPS).then_inc(pool_const, 1)
            pool.memset(eps[:, 1:2], EPS * B_DIM).then_inc(pool_const, 1)
            pool.iota(iota_c[:, :], [[1, P]], base=0, channel_multiplier=0,
                      allow_small_or_imprecise_dtypes=True).then_inc(pool_const, 1)
            pool.iota(dist[:, :], [[1, S]], base=-(S - P), channel_multiplier=-1,
                      allow_small_or_imprecise_dtypes=True).then_inc(pool_const, 1)
            step.n = 9
            pool.wait_ge(pool_const, 9)
            step(pool.affine_select(out=ident[:, :], in_=ident[:, :], compare_op=ALU.not_equal, fill=1.0, base=0,
                                    pattern=[[-1, P]], channel_multiplier=1))
            step(pool.affine_select(out=triu[:, :], in_=triu[:, :], compare_op=ALU.is_ge, fill=0.0, base=0,
                                    pattern=[[1, P]], channel_multiplier=-1))
            step(pool.affine_select(out=causal[:, :], in_=causal[:, :], compare_op=ALU.is_ge, fill=MASKED, base=0,
                                    pattern=[[-1, P]], channel_multiplier=1))
            for l in range(LEVELS):
                s_, nb = 2 ** l, P >> (l + 1)
                v = level[:, l, :].rearrange("p (b x s) -> p b x s", b=nb, x=2)[:, :, 1, :]
                step(pool.memset(v, 1.0))
                step(pool.affine_select(out=v, in_=v, compare_op=ALU.is_ge, fill=0.0, base=0,
                                        pattern=[[-2 * s_, nb], [0, s_]], channel_multiplier=1))
                step(pool.affine_select(out=v, in_=v, compare_op=ALU.is_ge, fill=0.0, base=s_ - 1,
                                        pattern=[[2 * s_, nb], [0, s_]], channel_multiplier=-1))
            assert step.n == POOL_CONSTS
            step = Steps(pool, pool_c)
            pool.wait_ge(proj_out, N_SMALL)
            pool.memset(raw[:, :, 0:CONV_W - 1], 0.0).then_inc(raw_pad, 1)
            pool.tensor_scalar(iw_s[:, :, :], small[:, :, 128:132], IDX_SCALE, None, ALU.mult).then_inc(iws_done, 1)
            pool.wait_ge(iws_done, 1)
            for k, qb in enumerate(QBS):
                n = P * (qb + 1)
                if k >= 2:
                    pool.wait_ge(topk_done, k - 1)
                for h in range(IDX_HEADS):
                    i = k * IDX_HEADS + h
                    pool.wait_ge(idx_relu, i + 1)
                    wcol = iw_s[:, qb, h:h + 1]
                    if h == 0:
                        pool.tensor_scalar(score[k % 2][:, 0:n], relu[i % 2][:, 0:n], wcol, None,
                                           ALU.mult).then_inc(idx_acc, 1)
                    else:
                        pool.wait_ge(idx_acc, i)
                        step(pool.tensor_scalar(weighed[:, 0:n], relu[i % 2][:, 0:n], wcol, None, ALU.mult))
                        pool.tensor_tensor(score[k % 2][:, 0:n], score[k % 2][:, 0:n], weighed[:, 0:n],
                                           ALU.add).then_inc(idx_acc, 1)
                pool.wait_ge(idx_acc, (k + 1) * IDX_HEADS)
                pool.tensor_tensor(score[k % 2][:, n - P:n], score[k % 2][:, n - P:n], causal[:, :],
                                   ALU.add).then_inc(score_done, 1)
            delta_pool(pool, step)
            attention_pool(pool, step)
            experts_pool(pool, step)

        def xnorm_act(act, which, link):
            for hf in range(2):
                if which == 0:
                    act.wait_ge(x_in[hf], 16)
                else:
                    act.wait_ge(x1_done, 12 + 4 * hf)
                for t in range(4 * hf, 4 * hf + 4):
                    if 8 * which + t:
                        act.wait_ge(sq_done, 8 * which + t)
                    act.activation(njunk, xbuf[:, t, :], ACT.Square, accum_out=st[:, 0, 8 * which + t:8 * which + t + 1]
                                   ).then_inc(sq_done, 1)
                act.wait_ge(ms_done, 2 * which + hf + 1)
                o = slice(8 * which + 4 * hf, 8 * which + 4 * hf + 4)
                act.activation(st[:, 2, o], st[:, 1, o], ACT.Sqrt).then_inc(rt_done, 1)
            dst = (hT, h2T)[which]
            for j in range(0, 16, 2):
                hf, kc = j // 8, j % 8
                act.wait_ge(hx_mm, 16 * which + j + 1)
                act.wait_ge(mods_done, 2 * which + 2)
                act.activation(dst[:, kc, hf * HALF:(hf + 1) * HALF], bank(j % 4), ACT.Identity,
                               bias=mods[:, 2 * which + 1, kc:kc + 1],
                               scale=mods[:, 2 * which, kc:kc + 1]).then_inc(hx_act, 1)

        def xnorm_dve(dve, which, step):
            for hf in range(2):
                o = slice(8 * which + 4 * hf, 8 * which + 4 * hf + 4)
                dve.wait_ge(sq_done, 8 * which + 4 * (hf + 1))
                dve.tensor_scalar(st[:, 1, o], st[:, 0, o], 1.0 / D, EPS, ALU.mult, ALU.add).then_inc(ms_done, 1)
                dve.wait_ge(rt_done, 2 * which + hf + 1)
                dve.wait_ge(ms_done, 2 * which + hf + 1)
                step(dve.reciprocal(st[:, 3, o], st[:, 2, o]))
                step(dve.tensor_tensor(st[:, 4, o], st[:, 3, o], st[:, 3, o], ALU.mult))
                step(dve.tensor_tensor(st[:, 4, o], st[:, 4, o], st[:, 1, o], ALU.mult))
                step(dve.tensor_scalar(st[:, 4, o], st[:, 4, o], -0.5, 1.5, ALU.mult, ALU.add))
                step(dve.tensor_tensor(st[:, 5, o], st[:, 4, o], st[:, 3, o], ALU.mult))
                if which:
                    dve.wait_ge(x1_out[hf], 16)
                for t in range(4 * hf, 4 * hf + 4):
                    dve.tensor_scalar(xbuf[:, t, :], xbuf[:, t, :], st[:, 5, 8 * which + t:8 * which + t + 1], None,
                                      ALU.mult).then_inc(xn_done, 1)
            dst = (hT, h2T)[which]
            for j in range(1, 16, 2):
                hf, kc = j // 8, j % 8
                dve.wait_ge(hx_mm, 16 * which + j + 1)
                dve.wait_ge(mods_done, 2 * which + 2)
                dve.tensor_scalar(dst[:, kc, hf * HALF:(hf + 1) * HALF], bank(j % 4),
                                  mods[:, 2 * which, kc:kc + 1], mods[:, 2 * which + 1, kc:kc + 1],
                                  ALU.mult, ALU.add).then_inc(hx_dve, 1)

        def xnorm_pe(pe, which):
            for j in range(16):
                hf, kc = j // 8, j % 8
                pe.wait_ge(xn_done, 8 * which + 4 * hf + 4)
                if j >= 4:
                    pe.wait_ge(hx_dve if j % 2 else hx_act, 8 * which + (j - 4) // 2 + 1)
                for q in range(4):
                    ins = pe.transpose(bank(j % 4)[:, q * P:(q + 1) * P],
                                       xbuf[:, 4 * hf + q, kc * P:(kc + 1) * P], ident[:, :])
                ins.then_inc(hx_mm, 1)

        def ada_cols_pe(pe, m, name, n0):
            for i in range(2):
                w = weights(pe, seg0[name] + i)
                for j in range(4):
                    for kc in range(KC):
                        ins = pe.matmul(bank(6 + m % 2)[:, m * KC + 4 * i + j:m * KC + 4 * i + j + 1],
                                        w[:, kc, j * P:(j + 1) * P], c_sb[:, kc:kc + 1],
                                        start=(kc == 0), stop=(kc == KC - 1))
                ins.then_inc(ada_mm, 1)

        def ada_cols_dve(dve, m, part, n0):
            dve.wait_ge(ada_mm, n0 + 2)
            dve.scalar_tensor_tensor(out=mods[:, m, :], in0=bank(6 + m % 2)[:, m * KC:(m + 1) * KC],
                                     scalar=1.0 if m % 2 == 0 else 0.0, in1=b_sb[:, part * KC:(part + 1) * KC],
                                     op0=ALU.add, op1=ALU.add).then_inc(mods_done, 1)

        njunk = Region(R4 + D).take(D)

        @block.scalar
        def _(act):
            for hf in range(2):
                act.dma_start(xbuf[:, 4 * hf:4 * hf + 4, :], x_tiles[:, 4 * hf:4 * hf + 4, :]).then_inc(x_in[hf], 16)
            act.wait_ge(consts_in, CONSTS)
            act.activation(c_sb[:, :], c_sb[:, :], ACT.Silu).then_inc(silu_c, 1)
            xnorm_act(act, 0, None)
            act.wait_ge(pool_const, POOL_CONSTS)
            act.wait_ge(hx_mm, 16)

            def index_relus(k):
                qb = QBS[k]
                n = P * (qb + 1)
                for h in range(IDX_HEADS):
                    i = k * IDX_HEADS + h
                    act.wait_ge(idx_mm, i + 1)
                    if i >= 2:
                        act.wait_ge(idx_acc, i - 1)
                    act.activation(relu[i % 2][:, 0:n], pair[2 + i % 2][:, 0:n], ACT.Relu).then_inc(idx_relu, 1)

            for n, (kind, seg, t, h) in enumerate(jobs):
                for k, at in enumerate(IDX_AT):
                    if at == n:
                        index_relus(k)
                act.wait_ge(proj_mm, n + 1)
                b = bank(n % 4)
                if kind == "index":
                    act.activation(iqT[:, t, h * HALF:(h + 1) * HALF], b, ACT.Copy).then_inc(proj_out, 1)
                elif kind == "small":
                    act.activation(small[:, t, :], b[:, 0:140], ACT.Copy).then_inc(proj_out, 1)
                elif kind == "qkv":
                    lo = CONV_W - 1 + h * HALF
                    act.activation(raw[:, t, lo:lo + HALF], b, ACT.Copy).then_inc(proj_out, 1)
                elif kind == "z":
                    act.activation(z[:, t, :], b, ACT.Silu).then_inc(proj_out, 1)
                else:
                    i = n - (len(jobs) - 2 * NT)
                    if i >= 2:
                        act.wait_ge(aq_out[i % 2], 16 * (i // 2))
                    act.activation(aq_stage[i % 2], b, ACT.Copy).then_inc(proj_out, 1)
                    act.wait_ge(proj_out, n + 1)
                    act.dma_start(aq_dram[t * P:(t + 1) * P, h * HALF:(h + 1) * HALF],
                                  aq_stage[i % 2]).then_inc(aq_out[i % 2], 16)
            for i in range(2):
                act.wait_ge(aq_out[i], 16 * NT)
            link = Steps(act, act_c)
            delta_act(act, link)
            attention_act(act, link)
            xnorm_act(act, 1, link)
            search_act(act, link)
            gates_act(act, link)
            experts_act(act, link)

        @block.tensor
        def _(pe):
            pe.wait_ge(pool_const, POOL_CONSTS)
            pe.wait_ge(silu_c, 1)
            ada_cols_pe(pe, 0, "scale1", 0)
            ada_cols_pe(pe, 1, "shift1", 2)
            xnorm_pe(pe, 0)

            def index_logits(k):
                qb = QBS[k]
                n = P * (qb + 1)
                for h in range(IDX_HEADS):
                    i = k * IDX_HEADS + h
                    if i >= 2:
                        pe.wait_ge(idx_relu, i - 1)
                    lo = IDX_DIM * (h % 2)
                    for c0 in range(0, n, HALF):
                        w = min(HALF, n - c0)
                        ins = pe.matmul(pair[2 + i % 2][:, c0:c0 + w],
                                        iqT[lo:lo + IDX_DIM, h // 2, qb * P:(qb + 1) * P],
                                        iqT[lo:lo + IDX_DIM, 2, c0:c0 + w], start=True, stop=True)
                    ins.then_inc(idx_mm, 1)

            pe.wait_ge(hx_act, 8)
            pe.wait_ge(hx_dve, 8)
            for n, (kind, seg, t, h) in enumerate(jobs):
                for k, at in enumerate(IDX_AT):
                    if at == n:
                        if k == 0:
                            pe.wait_ge(proj_out, 6)
                        index_logits(k)
                w = weights(pe, seg)
                if n >= 4:
                    pe.wait_ge(proj_out, n - 3)
                b = bank(n % 4)
                for kc in range(KC):
                    se = {"start": kc == 0, "stop": kc == KC - 1}
                    if kind in ("index", "qkv"):
                        c0 = (t % 4) * P
                        ins = pe.matmul(b, w[:, kc, c0:c0 + P], hT[:, kc, h * HALF:(h + 1) * HALF], **se)
                    else:
                        wd = 140 if kind == "small" else HALF
                        ins = pe.matmul(b[:, 0:wd], hT[:, kc, t * P:(t + 1) * P], w[:, kc, 0:wd], **se)
                ins.then_inc(proj_mm, 1)
            delta_pe(pe)
            attention_pe(pe)
            residual_pe(pe)
            search_pe(pe)
            gates_pe(pe)
            experts_pe(pe)

        @block.vector
        def _(dve):
            step = Steps(dve, dve_c)
            dve.wait_ge(silu_c, 1)
            dve.tensor_copy(c_rep[:, :, :], c_sb[:, :].unsqueeze(2).broadcast_to([P, KC, P])).then_inc(c_wide, 1)
            ada_cols_dve(dve, 0, 1, 0)
            ada_cols_dve(dve, 1, 0, 2)
            xnorm_dve(dve, 0, step)
            for k, qb in enumerate(QBS):
                n = P * (qb + 1)
                s_ = score[k % 2][:, 0:n]
                dve.wait_ge(score_done, k + 1)
                for _ in range(TOPK // 8):
                    step(dve.max(top8, s_))
                    step(dve.match_replace(out=s_, in_to_replace=top8, in_values=s_, imm_value=TAKEN))
                dve.tensor_scalar(mask[:, MOFF[qb]:MOFF[qb + 1]], s_, TAKEN / 2, MASKED, ALU.is_gt,
                                  ALU.mult).then_inc(topk_done, 1)
            dve.wait_ge(pool_const, POOL_CONSTS)
            step(dve.tensor_copy(mask[:, 0:P], causal[:, :]))
            step(dve.memset(mask[:, P:2 * P], 0.0))
            dve.tensor_copy(mask[:, 2 * P:3 * P], causal[:, :]).then_inc(topk_done, 1)
            delta_dve(dve, step)
            attention_dve(dve, step)
            residual_dve(dve, step)
            search_dve(dve, step)
            gates_dve(dve, step)
            experts_dve(dve, step)


_INS = ["x", "c_col", "w_ada", "b_col", "b_gate", "w_in", "q_gain_col", "k_gain", "w_uv", "conv_col", "a_log",
        "dt_bias", "gdn_gain", "w_out", "w_query", "subT", "uT", "v_tab"]


def laid_out(x, c, w_ada, b_ada, w_in, q_gain, k_gain, w_uv, conv_w, a_log, dt_bias, gdn_gain, w_out,
             w_query, sub_keys, u_tab, v_tab):
    def arr(a):
        return np.ascontiguousarray(a)
    return {
        "x": arr(x),
        "c_col": arr(np.asarray(c).reshape(KC, P).T),
        "w_ada": arr(w_ada[0]),
        "b_col": arr(np.asarray(b_ada).reshape(48, P).T),
        "b_gate": arr(np.asarray(b_ada).reshape(6, D)[[2, 5]]),
        "w_in": arr(w_in[0]),
        "q_gain_col": arr(np.asarray(q_gain).reshape(P, 1)),
        "k_gain": arr(k_gain),
        "w_uv": arr(w_uv),
        "conv_col": arr(np.asarray(conv_w).reshape(CONV_W, 12, P).transpose(2, 1, 0)),
        "a_log": arr(a_log),
        "dt_bias": arr(dt_bias),
        "gdn_gain": arr(gdn_gain),
        "w_out": arr(w_out[0]),
        "w_query": arr(w_query[0]),
        "subT": arr(np.asarray(sub_keys).reshape(16, NKEYS, P).transpose(2, 0, 1)),
        "uT": arr(np.asarray(u_tab).reshape(NKEYS, NKEYS, KC, P).transpose(1, 3, 2, 0)),
        "v_tab": arr(np.asarray(v_tab).reshape(NKEYS, NKEYS, D)),
    }


def kernel(x, c, w_ada, b_ada, w_in, q_gain, k_gain, w_uv, conv_w, a_log, dt_bias, gdn_gain, w_out,
           w_query, sub_keys, u_tab, v_tab):
    import concourse.bacc as bacc
    from concourse.bass_utils import run_bass_kernel_spmd

    nc = bacc.Bacc("TRN2", target_bir_lowering=False, num_devices=1)
    data = laid_out(x, c, w_ada, b_ada, w_in, q_gain, k_gain, w_uv, conv_w, a_log, dt_bias, gdn_gain, w_out,
                    w_query, sub_keys, u_tab, v_tab)
    args = [nc.dram_tensor(n, data[n].shape, F32, kind="ExternalInput").ap() for n in _INS]
    out = nc.dram_tensor("out", [S, D], F32, kind="ExternalOutput").ap()
    layer(nc, *args, out)
    r = run_bass_kernel_spmd(nc, [data], core_ids=[0])
    return np.asarray(r.results[0]["out"]).reshape(1, S, D)
```

```python
from contextlib import ExitStack

import numpy as np

import concourse.bass as bass
from concourse import mybir

F32 = mybir.dt.float32
BF16 = mybir.dt.bfloat16
F16 = mybir.dt.float16
U32 = mybir.dt.uint32
ALU = mybir.AluOpType
ACT = mybir.ActivationFunctionType
AX = mybir.AxisListType

P = 128
S = 1024
D = 1024
NT = S // P
KC = D // P
HALF = 512
EPS = 1e-6
A_HEADS, A_LAT, A_VDIM = 8, 128, 64
IDX_HEADS, IDX_DIM, TOPK = 4, 64, 256
B_HEADS, B_DIM, CONV_W = 4, 128, 4
PEER_HEADS, NKEYS, PEER_TOPK = 8, 128, 16
SPLITS = (A_HEADS * A_LAT, A_LAT, IDX_HEADS * IDX_DIM, IDX_DIM, IDX_HEADS,
          B_HEADS * B_DIM, B_HEADS * B_DIM, B_HEADS * B_DIM, B_HEADS * B_DIM, B_HEADS, B_HEADS)
(AQ, AKV, IQ, IK, IW, BQ, BK, BV, BZ, BA, BB) = (int(o) for o in np.cumsum((0,) + SPLITS[:-1]))
MASKED = -1e30
TAKEN = -3e38
ATT_SCALE = A_LAT ** -0.5
IDX_SCALE = IDX_DIM ** -0.5 * IDX_HEADS ** -0.5
SLOPES = [2.0 ** (-8.0 * (h + 1) / A_HEADS) for h in range(A_HEADS)]
QBS = list(range(2, NT))
LEVELS = 7
G_TOK = 64
G_BLOCKS = S // G_TOK
SG = 4
NSG = NKEYS // SG
SCALE_U, SCALE_H, SCALE_V, SCALE_A, SCALE_G = 64.0, 16.0, 64.0, 16.0, 32768.0
POOL_CONSTS = 12 + 3 * LEVELS


def weight_segments(w_ada, w_in, w_out, w_query):
    def cols(w, lo, n):
        return w.rearrange("(kc p) n -> p kc n", p=P)[:, :, lo:lo + n]

    def ada(part):
        return [[(0, cols(w_ada, part * D + i * HALF, HALF))] for i in range(2)]

    def whole(w, lo, n):
        return [[(0, cols(w, lo + i * HALF, HALF))] for i in range(n // HALF)]

    segs, first = [], {}

    def add(name, more):
        first[name] = len(segs)
        segs.extend(more)

    add("scale1", ada(1))
    add("shift1", ada(0))
    add("index", [[(0, cols(w_in, IQ, 256)), (256, cols(w_in, IK, 64)), (320, cols(w_in, IK, 64))]])
    add("small", [[(0, cols(w_in, AKV, 128)), (128, cols(w_in, IW, 4)), (132, cols(w_in, BA, 8))]])
    add("qkv", whole(w_in, BQ, 3 * HALF))
    add("z", whole(w_in, BZ, HALF))
    add("aq", whole(w_in, AQ, 2 * HALF))
    add("gate1", ada(2))
    add("out", whole(w_out, 0, D))
    add("scale2", ada(4))
    add("shift2", ada(3))
    add("query", whole(w_query, 0, 4 * HALF))
    add("gate2", ada(5))
    return segs, first


def layer(nc, x, c_col, w_ada, b_col, b_gate, w_in, q_gain_col, k_gain, w_uv, conv_col, a_log,
          dt_bias, gdn_gain, w_out, w_query, subT, uT, v_tab, out):
    with ExitStack() as ctx:
        def sem(name):
            return ctx.enter_context(nc.semaphore(name))

        def sb(name, shape, dt=F32):
            return ctx.enter_context(nc.sbuf_tensor(name, shape, dt))

        aq_dram = nc.dram_tensor("aq_spill", [S, D], F32).ap()
        x1_dram = nc.dram_tensor("x1_spill", [S, D], F32).ap()
        e_dram = nc.dram_tensor("gelus", [NKEYS, P, S], F32).ap()
        g_dram = nc.dram_tensor("gates", [G_BLOCKS, P, NKEYS, G_TOK], F32).ap()

        pair = [ctx.enter_context(nc.psum_tensor(f"pair{i}", [P, 2 * HALF], F32)) for i in range(4)]

        def bank(i):
            return pair[i // 2][:, (i % 2) * HALF:(i % 2 + 1) * HALF]

        ident = sb("ident", [P, P])
        ones = sb("ones", [P, P])
        triu = sb("triu", [P, P])
        causal = sb("causal", [P, P])
        level = sb("level", [P, LEVELS, P])
        iota_c = sb("iota_c", [P, P])
        dist = sb("dist", [P, S])
        eps = sb("eps", [P, 2])
        c_sb = sb("c_sb", [P, KC])
        c_rep = sb("c_rep", [P, KC, P])
        mods = sb("mods", [P, 4, KC])
        b_sb = sb("b_sb", [P, 48])
        st = sb("st", [P, 8, 16])
        qg = sb("qg", [P, 1])
        kg = sb("kg", [P, A_LAT])
        gg = sb("gg", [P, B_DIM])
        conv_sb = sb("conv_sb", [P, 12, CONV_W])
        al = sb("al", [P, B_HEADS])
        dtb = sb("dtb", [P, B_HEADS])
        wuv = sb("wuv", [P, A_HEADS, A_VDIM])
        NARENA = (nc.sbuf_bytes_remaining - 256) // 4
        NARENA -= NARENA % 8
        arena = sb("arena", [P, NARENA])

        class Region:
            def __init__(self, start):
                self.at = start

            def take(self, *shape, dt=F32):
                n = int(np.prod(shape))
                words = n if dt in (F32, U32) else n // 2
                v = arena[:, self.at:self.at + words]
                self.at += words
                assert self.at <= NARENA, (self.at, NARENA)
                if dt is not F32:
                    v = v.bitcast(dt)
                if len(shape) == 2:
                    return v.rearrange("p (a b) -> p a b", a=shape[0])
                if len(shape) == 3:
                    return v.rearrange("p (a b c) -> p a b c", a=shape[0], b=shape[1])
                return v

        base = Region(0)
        hT = base.take(KC, S)
        mixT = hT
        wring = [base.take(KC, HALF) for _ in range(2)]
        R0 = base.at
        r = Region(R0)
        xbuf = r.take(NT, D)
        yacc = xbuf
        h2T = r.take(KC, S)
        R2 = r.at
        r = Region(R0)
        raw = r.take(12, CONV_W - 1 + S)
        z = r.take(NT, B_HEADS * B_DIM)
        small = r.take(NT, 140)
        MOFF = [P * qb * (qb + 1) // 2 for qb in range(NT + 1)]
        mask = r.take(MOFF[NT], dt=BF16)
        R3 = r.at
        iqT = r.take(3, S)
        aq_stage = [r.take(HALF) for _ in range(2)]
        relu = [r.take(S) for _ in range(2)]
        weighed = r.take(S)
        score = [r.take(S) for _ in range(2)]
        top8 = r.take(8)
        iw_s = r.take(NT, IDX_HEADS)
        r = Region(R3)
        HP = B_HEADS * P
        cv = [r.take(S) for _ in range(2)]
        norm = cv
        gates = r.take(16, NT * B_HEADS)
        growb = [cv[i][:, 0:HP] for i in range(2)]
        decayT = [cv[i][:, HP:2 * HP] for i in range(2)]
        spread = r.take(2, HP)
        invT = [r.take(HP) for _ in range(4)]
        attnT = [r.take(HP) for _ in range(4)]
        state = r.take(HP)
        resid = r.take(HP)
        vnew = r.take(HP)
        qse = r.take(HP)
        o_sb = r.take(HP)
        sqj = r.take(HP)
        yb = r.take(HP)
        ost = r.take(4, B_HEADS)
        r = Region(R0 - 2 * KC * HALF)
        kdec = [r.take(HP) for _ in range(4)]
        bv = [r.take(HP) for _ in range(4)]
        upper = [r.take(HP) for _ in range(2)]
        upper_s = [r.take(HP) for _ in range(2)]
        n1 = [r.take(HP) for _ in range(2)]
        inv = [r.take(HP) for _ in range(2)]
        assert r.at <= R0
        r = Region(R3)
        ktok = r.take(NT, A_LAT)
        kT = r.take(S)
        kst = r.take(4, NT)
        aqt = [r.take(A_HEADS, A_LAT) for _ in range(2)]
        qst = r.take(4, A_HEADS)
        sq_junk = r.take(A_LAT)
        r = Region(R0)
        qT = [r.take(A_HEADS, P) for _ in range(2)]
        inv_sum = r.take(A_HEADS)
        dm = r.take(S)
        bias = [r.take(S) for _ in range(2)]
        sc = [r.take(S) for _ in range(2)]
        pr = [r.take(S) for _ in range(2)]
        smax = r.take(3, A_HEADS)
        PT = r.take(NT, 4, P)
        oT = r.take(A_HEADS, P)
        ya = r.take(A_HEADS * A_VDIM)
        r = Region(R2)
        grow1 = r.take(D)
        grow2 = r.take(D)
        bg = r.take(2, D)
        gmix = [Region(R2 + 4 * D).take(HALF), Region(R2 + 4 * D + HALF).take(HALF)]
        R4 = r.at
        pqT = [r.take(4, S), Region(0).take(4, S)]
        sub = r.take(16, NKEYS)
        s_st = [r.take(HALF) for _ in range(2)]
        s_tmp = r.take(P)
        sh = r.take(NT, 16, PEER_TOPK)
        ih = r.take(NT, 16, PEER_TOPK)
        m_ix = r.take(4 * PEER_TOPK, dt=U32)
        r2 = Region(0)
        cand = r2.take(PEER_HEADS, 256)
        cand2 = r2.take(256)
        eq = r2.take(PEER_HEADS, PEER_TOPK, PEER_TOPK)
        cs = r2.take(PEER_HEADS, PEER_TOPK)
        ce = r2.take(PEER_HEADS, PEER_TOPK)
        ci = r2.take(PEER_HEADS * PEER_TOPK, dt=U32)
        cab = r2.take(2, PEER_HEADS * PEER_TOPK, dt=U32)
        cabf = r2.take(2, PEER_HEADS * PEER_TOPK)
        sel = [r2.take(3, PEER_HEADS * PEER_TOPK) for _ in range(2)]
        gs = r2.take(PEER_HEADS)
        assert r2.at <= R0 - KC * HALF * 2
        r = Region(R4)
        selT = r.take(4, S)
        oh = r.take(4, 2 * 4 * P, dt=F16)
        oh2 = r.take(16, 2, P, dt=F16)
        g_hi = r.take(S, dt=F16)
        gst = [Region(i * NKEYS * G_TOK).take(NKEYS, G_TOK) for i in range(2)]
        r = Region(R0)
        h_hi, h_lo = r.take(KC, S, dt=F16), r.take(KC, S, dt=F16)
        u_raw = [r.take(KC, P) for _ in range(4)]
        u_split = [r.take(2, KC, P, dt=F16) for _ in range(2)]
        e_stage = [r.take(S) for _ in range(2)]
        assert r.at <= R2
        r = Region(0)
        e_sb = [r.take(S) for _ in range(SG)]
        v_raw = [r.take(D) for _ in range(SG)]
        x1_in_sb = Region(0).take(NT, D)
        g_sb = [r.take(G_BLOCKS, SG, G_TOK) for _ in range(2)]
        r.at += NT * D
        a_split = [r.take(SG, 2, S, dt=F16) for _ in range(2)]
        assert r.at <= R2
        r = Region(R2 + 2 * D)
        v_split = [r.take(SG, 2, D, dt=F16) for _ in range(2)]
        segs, seg0 = weight_segments(w_ada, w_in, w_out, w_query)
        NSEG = len(segs)

        consts_in = sem("consts_in")
        x_in = [sem(f"x_in{i}") for i in range(2)]
        x2_in = sem("x2_in")
        w_in_s = [sem(f"w_slot{i}") for i in range(2)]
        pool_const = sem("pool_const")
        silu_c = sem("silu_c")
        ada_mm = sem("ada_mm")
        ada_row = sem("ada_row")
        mods_done = sem("mods_done")
        sq_done = sem("sq_done")
        ms_done = sem("ms_done")
        rt_done = sem("rt_done")
        dve_c = sem("dve_c")
        pool_c = sem("pool_c")
        xn_done = sem("xn_done")
        hx_mm = sem("hx_mm")
        hx_act = sem("hx_act")
        hx_dve = sem("hx_dve")
        proj_mm = sem("proj_mm")
        proj_out = sem("proj_out")
        aq_out = [sem(f"aq_out{i}") for i in range(2)]
        raw_pad = sem("raw_pad")
        idx_mm = sem("idx_mm")
        idx_relu = sem("idx_relu")
        idx_acc = sem("idx_acc")
        score_done = sem("score_done")
        topk_done = sem("topk_done")
        late_in = sem("late_in")

        SEG_SMALL = seg0["small"]
        jobs = [("index", seg0["index"], f, h) for f in range(3) for h in range(2)]
        jobs += [("small", SEG_SMALL, t, 0) for t in range(NT)]
        N_SMALL = len(jobs)
        jobs += [("qkv", seg0["qkv"] + j // 4, j, h) for j in range(12) for h in range(2)]
        N_QKV = len(jobs)
        jobs += [("z", seg0["z"], t, 0) for t in range(NT)]
        jobs += [("aq", seg0["aq"] + i, t, i) for i in range(2) for t in range(NT)]
        IDX_AT = [N_SMALL, N_SMALL, N_SMALL + 4, N_SMALL + 8, N_SMALL + 14, N_SMALL + 21]
        SILU_AT, ROOT_AT = N_QKV + 3, N_QKV + 15
        assert ROOT_AT + 2 * B_HEADS < len(jobs)
        last_of = {}
        for n, job in enumerate(jobs):
            last_of[job[1]] = n + 1

        released = {}
        for name, n0 in (("scale1", 0), ("shift1", 2), ("gate1", 4), ("scale2", 6), ("shift2", 8), ("gate2", 10)):
            for i in range(2):
                released[seg0[name] + i] = (ada_mm, n0 + i + 1)
        for s_, n in last_of.items():
            released[s_] = (proj_mm, n)
        out_mm = sem("out_mm")
        q_mm = sem("q_mm")
        for i in range(2):
            released[seg0["out"] + i] = (out_mm, NT * (i + 1))
        for i in range(4):
            released[seg0["query"] + i] = (q_mm, 8 * (i + 1))

        slot_uses = [0, 0]
        seg_ready = []
        for n, parts in enumerate(segs):
            slot_uses[n % 2] += 16 * len(parts)
            seg_ready.append(slot_uses[n % 2])

        class Steps:
            def __init__(self, eng, s_):
                self.eng, self.sem, self.n = eng, s_, 0
                self.before, self.first = None, 0

            def __call__(self, ins):
                ins.then_inc(self.sem, 1)
                self.n += 1
                if self.before is None:
                    self.eng.wait_ge(self.sem, self.n)
                else:
                    self.eng.wait_ge(self.sem, self.before + (self.n - self.first))

            def enter(self, i, each):
                self.first, self.before, self.each = self.n, i * each + self.n, each

            def leave(self, times):
                assert self.n - self.first == self.each
                self.n, self.before = self.first + self.each * times, None

        def weights(pe, seg):
            pe.wait_ge(w_in_s[seg % 2], seg_ready[seg])
            return wring[seg % 2]

        block = ctx.enter_context(nc.Block())

        small_loads = [
            (c_sb[:, :], c_col), (b_sb[:, :], b_col), (qg[:, :], q_gain_col),
            (kg[:, :], k_gain.broadcast_to([P, A_LAT])), (gg[:, :], gdn_gain.broadcast_to([P, B_DIM])),
            (conv_sb[:, :, :], conv_col), (al[:, :], a_log.broadcast_to([P, B_HEADS])),
            (dtb[:, :], dt_bias.broadcast_to([P, B_HEADS])),
            (wuv[:, :, :], w_uv[0].rearrange("h r v -> r h v")),
        ]
        CONSTS = 16 * len(small_loads)
        x_tiles = x[0].rearrange("(t p) d -> p t d", p=P)

        conv_done = sem("conv_done")
        raw_done = sem("raw_done")
        l2_sq = sem("l2_sq")
        l2_mm = sem("l2_mm")
        l2_rt = sem("l2_rt")
        l2_done = sem("l2_done")
        gate_v = sem("gate_v")
        gate_s = sem("gate_s")
        gate_mm = sem("gate_mm")
        d_spread = sem("d_spread")
        d_pre = sem("d_pre")
        d_pre2 = sem("d_pre2")
        d_dif = sem("d_dif")
        d_exp = sem("d_exp")
        d_upper = sem("d_upper")
        d_kv = sem("d_kv")
        d_us = sem("d_us")
        d_n1 = sem("d_n1")
        d_n1s = sem("d_n1s")
        d_dx = sem("d_dx")
        d_dy = sem("d_dy")
        d_invx = sem("d_invx")
        d_inv = sem("d_inv")
        d_ks = sem("d_ks")
        d_qs = sem("d_qs")
        d_res = sem("d_res")
        d_vn = sem("d_vn")
        d_vns = sem("d_vns")
        d_ds = sem("d_ds")
        d_state = sem("d_state")
        d_o = sem("d_o")
        d_osq = sem("d_osq")
        d_oms = sem("d_oms")
        d_ort = sem("d_ort")
        d_yb = sem("d_yb")
        d_yt = sem("d_yt")
        d_mix = sem("d_mix")
        H4 = B_HEADS
        LANES = [P, H4, P]

        def heads(ap):
            return ap.rearrange("p (h n) -> p h n", h=H4)

        def per_head(col):
            return col.unsqueeze(2).broadcast_to(LANES)

        def all_heads(tab):
            return tab.unsqueeze(1).broadcast_to(LANES)

        def hcol(h):
            return slice(h * P, (h + 1) * P)

        def chunk_of(j, c):
            return raw[:, j, CONV_W - 1 + c * P:CONV_W - 1 + (c + 1) * P]

        def gate(k, c=None):
            v = gates[:, k, :]
            return v if c is None else v[:, c * H4:(c + 1) * H4]

        (G_X, G_ABS, G_EXP, G_LN, G_POS, G_SP, G_G, G_BETA, G_CUM, G_ECUM, G_LAST, G_EDEC, G_ELAST, G_NBE,
         G_ALOG, G_DIF) = range(16)

        def conv_dve(dve, step):
            for j in range(12):
                if j >= 2:
                    dve.wait_ge(raw_done, j - 1)
                o = cv[j % 2]
                if j == 0:
                    dve.wait_ge(proj_out, N_QKV)
                step(dve.tensor_scalar(o, raw[:, j, 0:S], conv_sb[:, j, 0:1], None, ALU.mult))
                for w in range(1, CONV_W):
                    ins = dve.scalar_tensor_tensor(out=o, in0=raw[:, j, w:w + S], scalar=conv_sb[:, j, w:w + 1],
                                                   in1=o, op0=ALU.mult, op1=ALU.add)
                    if w < CONV_W - 1:
                        step(ins)
                    else:
                        ins.then_inc(conv_done, 1)
            for j in range(2 * H4):
                dve.wait_ge(l2_rt, j + 1)
                step(dve.reciprocal(norm[j % 2], norm[j % 2]))
                dve.tensor_tensor(raw[:, j, CONV_W - 1:], raw[:, j, CONV_W - 1:], norm[j % 2],
                                  ALU.mult).then_inc(l2_done, 1)

        def topk_round(dve, step, s_, best):
            step(dve.max(best, s_))
            step(dve.match_replace(out=s_, in_to_replace=best, in_values=s_, imm_value=TAKEN))

        def topk_mask(dve, qb, s_):
            dve.tensor_scalar(mask[:, MOFF[qb]:MOFF[qb + 1]], s_, TAKEN / 2, MASKED, ALU.is_gt,
                              ALU.mult).then_inc(topk_done, 1)

        late_score, late_top8 = mixT[:, 0, :], mixT[:, 1, 0:8]

        def delta_dve(dve, step):
            rounds = []

            def late_round(n=1):
                for _ in range(min(n, TOPK // 8 - len(rounds))):
                    if not rounds:
                        dve.wait_ge(late_in, 1)
                    rounds.append(1)
                    topk_round(dve, step, late_score, late_top8)

            t3 = [P, NT, H4]

            def g3(k):
                return gates[:, k, :].rearrange("p (t h) -> p t h", h=H4)
            step(dve.tensor_tensor(g3(G_X), small[:, :, 132:136], dtb[:, :].unsqueeze(1).broadcast_to(t3), ALU.add))
            step(dve.tensor_scalar(gate(G_POS), gate(G_X), 0.0, None, ALU.max))
            dve.scalar_tensor_tensor(out=gate(G_ABS), in0=gate(G_POS), scalar=2.0, in1=gate(G_X), op0=ALU.mult,
                                     op1=ALU.subtract).then_inc(gate_v, 1)
            dve.wait_ge(gate_s, 4)
            step(dve.tensor_tensor(gate(G_SP), gate(G_LN), gate(G_POS), ALU.add))
            step(dve.tensor_scalar(gate(G_SP), gate(G_SP), -1.0, None, ALU.mult))
            step(dve.tensor_tensor(g3(G_G), g3(G_SP), gates[:, G_ALOG, 0:H4].unsqueeze(1).broadcast_to(t3), ALU.mult))
            step(dve.tensor_scalar(gate(G_BETA), gate(G_BETA), 1.0, None, ALU.add))
            dve.reciprocal(gate(G_BETA), gate(G_BETA)).then_inc(gate_v, 1)
            dve.wait_ge(gate_s, 8)
            dve.tensor_tensor(gate(G_DIF), gate(G_LAST), gate(G_CUM), ALU.subtract).then_inc(gate_v, 1)
            dve.wait_ge(gate_v, 2)
            step(dve.tensor_tensor(gate(G_NBE), gate(G_BETA), gate(G_ECUM), ALU.mult))
            step(dve.tensor_scalar(gate(G_NBE), gate(G_NBE), -1.0, None, ALU.mult))
            step(dve.memset(state, 0.0))

            def pre(c):
                x = c % 2
                dve.wait_ge(d_pre, 3 * c + 1)
                if c == 0:
                    dve.wait_ge(gate_s, 9)
                    dve.wait_ge(l2_done, 2 * H4)
                for h in range(H4):
                    ins = dve.tensor_scalar(growb[x][:, hcol(h)], bank(3 * x)[:, hcol(h)],
                                            gate(G_CUM, c)[:, h:h + 1], 0.0, ALU.subtract, ALU.min)
                ins.then_inc(d_dif, 1)
                step(dve.tensor_copy(heads(inv[x]), all_heads(ident[:, :])))
                step(dve.tensor_copy(heads(invT[c % 4]), all_heads(ident[:, :])))
                dve.wait_ge(d_exp, c + 1)
                step(dve.tensor_tensor(heads(decayT[x]), heads(decayT[x]), all_heads(triu[:, :]), ALU.mult))
                dve.wait_ge(d_pre, 3 * c + 3)
                step(dve.tensor_tensor(upper[x], bank(3 * x + 2), decayT[x], ALU.mult))
                dve.tensor_tensor(upper[x], upper[x], bank(3 * x + 1), ALU.mult).then_inc(d_upper, 1)

            def pre2(c):
                x = c % 2
                dve.wait_ge(d_pre2, 3 * c + 3)
                dve.tensor_tensor(attnT[c % 4], bank(3 * x), decayT[x], ALU.mult)
                dve.tensor_tensor(heads(kdec[c % 4]), heads(bank(3 * x + 1)), per_head(gate(G_EDEC, c)), ALU.mult)
                dve.tensor_tensor(heads(bv[c % 4]), heads(bank(3 * x + 2)), per_head(gate(G_BETA, c)), ALU.mult
                                  ).then_inc(d_kv, 1)

            def level_x(p, l):
                late_round()
                for x in range(2):
                    i = 14 * p + 2 * l + x
                    ix = 12 * p + 2 * l + x
                    y_ = invT[(2 * p + x) % 4]
                    if l < LEVELS - 1:
                        dve.wait_ge(d_dx, ix + 1)
                        dve.tensor_tensor(inv[x], inv[x], bank(3 * x + 1), ALU.subtract).then_inc(d_invx, 1)
                    dve.wait_ge(d_dy, i + 1)
                    dve.tensor_tensor(y_, y_, bank(3 * x + 2), ALU.subtract).then_inc(d_inv, 1)

            def rec(c, piece):
                if piece == "ks":
                    dve.wait_ge(d_ks, 2 * c + 2)
                    for h in range(H4):
                        ins = dve.scalar_tensor_tensor(out=resid[:, hcol(h)], in0=bank(6)[:, hcol(h)],
                                                       scalar=gate(G_NBE, c)[:, h:h + 1], in1=bv[c % 4][:, hcol(h)],
                                                       op0=ALU.mult, op1=ALU.add)
                    ins.then_inc(d_res, 1)
                elif piece == "ds":
                    dve.wait_ge(d_ds, 2 * c + 1)
                    for h in range(H4):
                        ins = dve.scalar_tensor_tensor(out=state[:, hcol(h)], in0=state[:, hcol(h)],
                                                       scalar=gate(G_ELAST, c)[:, h:h + 1], in1=bank(7)[:, hcol(h)],
                                                       op0=ALU.mult, op1=ALU.add)
                    ins.then_inc(d_state, 1)
                    dve.wait_ge(d_qs, c + 1)
                    dve.wait_ge(d_ds, 2 * c + 2)
                    if c:
                        dve.wait_ge(d_yb, c)
                    dve.tensor_tensor(o_sb, qse, bank(6), ALU.add).then_inc(d_o, 1)
                    step(dve.tensor_tensor(heads(z[:, c, :]), heads(z[:, c, :]), all_heads(gg[:, :]), ALU.mult))
                elif piece == "n1":
                    dve.wait_ge(d_osq, c * H4 + H4)
                    dve.tensor_scalar(ost[:, 1, :], ost[:, 0, :], 1.0 / B_DIM, EPS, ALU.mult, ALU.add
                                      ).then_inc(d_oms, 1)
                elif piece == "n2":
                    dve.wait_ge(d_ort, c + 1)
                    step(dve.reciprocal(ost[:, 3, :], ost[:, 2, :]))
                    if c:
                        dve.wait_ge(d_yt, c)
                    for h in range(H4):
                        ins = dve.scalar_tensor_tensor(out=yb[:, hcol(h)], in0=o_sb[:, hcol(h)],
                                                       scalar=ost[:, 3, h:h + 1], in1=z[:, c, hcol(h)],
                                                       op0=ALU.mult, op1=ALU.mult)
                    ins.then_inc(d_yb, 1)

            delta_pairs(pre, pre2, level_x, rec)
            late_round(TOPK // 8)
            topk_mask(dve, NT - 1, late_score)

        def conv_silu(act, j):
            act.wait_ge(conv_done, j + 1)
            act.activation(raw[:, j, CONV_W - 1:], cv[j % 2], ACT.Silu).then_inc(raw_done, 1)

        def l2_root(act, j):
            if j >= 2:
                act.wait_ge(l2_done, j - 1)
            else:
                act.wait_ge(raw_done, 12)
            act.activation(norm[j % 2], raw[:, j, CONV_W - 1:], ACT.Square).then_inc(l2_sq, 1)
            act.wait_ge(l2_mm, j + 1)
            q = j < H4
            act.activation(norm[j % 2], pair[2 + j % 2][:, :], ACT.Sqrt, scale=float(B_DIM) if q else 1.0,
                           bias=eps[:, 1:2] if q else eps[:, 0:1]).then_inc(l2_rt, 1)

        def l2_sum(pe, j):
            pe.wait_ge(l2_sq, j + 1)
            if j >= 2:
                pe.wait_ge(l2_rt, j - 1)
            else:
                pe.wait_ge(idx_relu, len(QBS) * IDX_HEADS)
            for hf in range(2):
                ins = pe.matmul(pair[2 + j % 2][:, hf * HALF:(hf + 1) * HALF], ones[:, :],
                                norm[j % 2][:, hf * HALF:(hf + 1) * HALF], start=True, stop=True)
            ins.then_inc(l2_mm, 1)

        def delta_act(act):
            act.wait_ge(gate_v, 1)
            act.activation(gate(G_EXP), gate(G_ABS), ACT.Exp, scale=-1.0).then_inc(gate_s, 1)
            act.activation(gates[:, G_ALOG, 0:H4], al[:, :], ACT.Exp).then_inc(gate_s, 1)
            act.activation(gates[:, G_BETA, :].rearrange("p (t h) -> p t h", h=H4), small[:, :, 136:140], ACT.Exp,
                           scale=-1.0).then_inc(gate_s, 1)
            act.wait_ge(gate_s, 1)
            act.activation(gate(G_LN), gate(G_EXP), ACT.Ln, bias=ones[:, 0:1]).then_inc(gate_s, 1)
            act.wait_ge(gate_mm, 1)
            act.activation(gate(G_CUM), bank(0)[:, 0:32], ACT.Copy).then_inc(gate_s, 1)
            act.activation(gate(G_LAST), bank(0)[:, 32:64], ACT.Copy).then_inc(gate_s, 1)
            act.activation(gate(G_ECUM), bank(0)[:, 0:32], ACT.Exp).then_inc(gate_s, 1)
            act.activation(gate(G_ELAST), bank(0)[:, 32:64], ACT.Exp).then_inc(gate_s, 1)
            act.wait_ge(gate_v, 3)
            act.activation(gate(G_EDEC), gate(G_DIF), ACT.Exp).then_inc(gate_s, 1)
            def pre(c):
                act.wait_ge(d_dif, c + 1)
                act.activation(decayT[c % 2], growb[c % 2], ACT.Exp).then_inc(d_exp, 1)

            def level_x(p, l):
                for x in range(2):
                    act.wait_ge(d_n1, 14 * p + 2 * l + x + 1)
                    act.activation(n1[x], bank(3 * x), ACT.Copy).then_inc(d_n1s, 1)

            def rec(c, piece):
                if piece == "ks":
                    act.wait_ge(d_ks, 2 * c + 2)
                    if c:
                        act.wait_ge(d_o, c)
                    for h in range(H4):
                        ins = act.activation(qse[:, hcol(h)], bank(7)[:, hcol(h)], ACT.Copy,
                                             scale=gate(G_ECUM, c)[:, h:h + 1])
                    ins.then_inc(d_qs, 1)
                elif piece == "vn":
                    act.wait_ge(d_vn, c + 1)
                    act.activation(vnew, bank(6), ACT.Copy).then_inc(d_vns, 1)
                elif piece == "n1":
                    act.wait_ge(d_o, c + 1)
                    for h in range(H4):
                        if c + h:
                            act.wait_ge(d_osq, c * H4 + h)
                        act.activation(sqj[:, hcol(h)], o_sb[:, hcol(h)], ACT.Square,
                                       accum_out=ost[:, 0, h:h + 1]).then_inc(d_osq, 1)
                elif piece == "n2":
                    act.wait_ge(d_oms, c + 1)
                    act.activation(ost[:, 2, :], ost[:, 1, :], ACT.Sqrt).then_inc(d_ort, 1)
                elif piece == "yt":
                    act.wait_ge(d_yt, c + 1)
                    act.activation(mixT[:, H4:2 * H4, c * P:(c + 1) * P], heads(bank(7)), ACT.Copy).then_inc(d_mix, 1)

            delta_pairs(pre, None, level_x, rec)

        def delta_pool(pool, step):
            pool.wait_ge(gate_v, 2)

            def pre(c):
                if c:
                    pool.wait_ge(d_pre, 3 * c - 1)
                pool.tensor_copy(heads(spread[:, 0, :]), per_head(gate(G_G, c))).then_inc(d_spread, 1)
                pool.tensor_copy(heads(spread[:, 1, :]), per_head(gate(G_BETA, c))).then_inc(d_spread, 1)

            def level_x(p, l):
                for x in range(2):
                    i = 14 * p + 2 * l + x
                    if l == 0:
                        pool.wait_ge(d_upper, 2 * p + x + 1)
                    if i >= 2:
                        pool.wait_ge(d_n1, i - 1)
                    pool.tensor_tensor(heads(upper_s[x]), heads(upper[x]), all_heads(level[:, l, :]),
                                       ALU.mult).then_inc(d_us, 1)

            delta_pairs(pre, None, level_x, None)

        BESIDE = [[(0, "ks")], [(0, "vn")], [(0, "ds")], [(1, "ks"), (0, "n1")], [(1, "vn"), (0, "n2")],
                  [(0, "yt"), (1, "ds")], [(1, "n1")]]
        AFTER = [(1, "n2"), (1, "yt")]

        def delta_pairs(pre, pre2, level_x, rec):
            for p in range(NT // 2 + 1):
                if p < NT // 2:
                    for x in range(2):
                        pre(2 * p + x)
                    for x in range(2):
                        if pre2:
                            pre2(2 * p + x)
                for l in range(LEVELS):
                    if p < NT // 2:
                        level_x(p, l)
                    for x, piece in BESIDE[l] if p and rec else ():
                        rec(2 * p - 2 + x, piece)
                for x, piece in AFTER if p and rec else ():
                    rec(2 * p - 2 + x, piece)

        def delta_pe(pe):
            pe.wait_ge(gate_v, 2)
            pe.wait_ge(proj_out, len(jobs))
            pe.matmul(bank(0)[:, 0:32], triu[:, :], gate(G_G), start=True, stop=True)
            pe.matmul(bank(0)[:, 32:64], ones[:, :], gate(G_G), start=True, stop=True).then_inc(gate_mm, 1)
            def pre(c):
                x = c % 2
                pe.wait_ge(d_spread, 2 * c + 2)
                if c == 0:
                    pe.wait_ge(gate_s, 9)
                    pe.wait_ge(l2_done, 2 * H4)
                elif c >= 2:
                    pe.wait_ge(d_inv, 14 * (c // 2))
                for i, rhs in enumerate((triu, ident)):
                    for h in range(H4):
                        ins = pe.matmul(bank(3 * x + i)[:, hcol(h)], spread[:, i, hcol(h)], rhs[:, :], start=True,
                                        stop=True)
                    ins.then_inc(d_pre, 1)
                for h in range(H4):
                    ins = pe.matmul(bank(3 * x + 2)[:, hcol(h)], chunk_of(H4 + h, c), chunk_of(H4 + h, c), start=True,
                                    stop=True)
                ins.then_inc(d_pre, 1)

            def pre2(c):
                x = c % 2
                pe.wait_ge(d_upper, c + 1)
                for h in range(H4):
                    ins = pe.matmul(bank(3 * x)[:, hcol(h)], chunk_of(H4 + h, c), chunk_of(h, c), start=True,
                                    stop=True)
                ins.then_inc(d_pre2, 1)
                for i, j0 in enumerate((H4, 2 * H4)):
                    for h in range(H4):
                        ins = pe.transpose(bank(3 * x + 1 + i)[:, hcol(h)], chunk_of(j0 + h, c), ident[:, :])
                    ins.then_inc(d_pre2, 1)

            def level_x(p, l):
                for x in range(2):
                    pe.wait_ge(d_us, 14 * p + 2 * l + x + 1)
                    if l:
                        pe.wait_ge(d_invx, 12 * p + 2 * (l - 1) + x + 1)
                    else:
                        pe.wait_ge(d_kv, 2 * p + x + 1)
                    for h in range(H4):
                        ins = pe.matmul(bank(3 * x)[:, hcol(h)], upper_s[x][:, hcol(h)], inv[x][:, hcol(h)],
                                        start=True, stop=True)
                    ins.then_inc(d_n1, 1)
                for x in range(2):
                    y_ = invT[(2 * p + x) % 4]
                    pe.wait_ge(d_n1s, 14 * p + 2 * l + x + 1)
                    if l:
                        pe.wait_ge(d_inv, 14 * p + 2 * (l - 1) + x + 1)
                    if l < LEVELS - 1:
                        for h in range(H4):
                            ins = pe.matmul(bank(3 * x + 1)[:, hcol(h)], y_[:, hcol(h)], n1[x][:, hcol(h)], start=True,
                                            stop=True)
                        ins.then_inc(d_dx, 1)
                    for h in range(H4):
                        ins = pe.matmul(bank(3 * x + 2)[:, hcol(h)], n1[x][:, hcol(h)], y_[:, hcol(h)], start=True,
                                        stop=True)
                    ins.then_inc(d_dy, 1)

            def rec(c, piece):
                if piece == "ks":
                    if c:
                        pe.wait_ge(d_state, c)
                        pe.wait_ge(d_o, c)
                    if c >= 2:
                        pe.wait_ge(d_mix, c - c % 2)
                    for i, j0 in enumerate((H4, 0)):
                        for h in range(H4):
                            ins = pe.matmul(bank(6 + i)[:, hcol(h)], chunk_of(j0 + h, c), state[:, hcol(h)],
                                            start=True, stop=True)
                        ins.then_inc(d_ks, 1)
                elif piece == "vn":
                    pe.wait_ge(d_res, c + 1)
                    pe.wait_ge(d_inv, 14 * (c // 2 + 1))
                    for h in range(H4):
                        ins = pe.matmul(bank(6)[:, hcol(h)], invT[c % 4][:, hcol(h)], resid[:, hcol(h)], start=True,
                                        stop=True)
                    ins.then_inc(d_vn, 1)
                elif piece == "ds":
                    pe.wait_ge(d_vns, c + 1)
                    pe.wait_ge(d_qs, c + 1)
                    for i, lhs in ((1, kdec), (0, attnT)):
                        if i:
                            if c % 2:
                                pe.wait_ge(d_mix, c)
                        for h in range(H4):
                            ins = pe.matmul(bank(6 + i)[:, hcol(h)], lhs[c % 4][:, hcol(h)], vnew[:, hcol(h)],
                                            start=True, stop=True)
                        ins.then_inc(d_ds, 1)
                elif piece == "yt":
                    pe.wait_ge(d_yb, c + 1)
                    if c % 2 == 0:
                        pe.wait_ge(d_qs, c + 2)
                    else:
                        pe.wait_ge(d_state, c + 1)
                    for h in range(H4):
                        ins = pe.transpose(bank(7)[:, hcol(h)], yb[:, hcol(h)], ident[:, :])
                    ins.then_inc(d_yt, 1)

            delta_pairs(pre, pre2, level_x, rec)

        a_ksq = sem("a_ksq")
        a_kms = sem("a_kms")
        a_krt = sem("a_krt")
        a_k = sem("a_k")
        a_ktr = sem("a_ktr")
        a_kT = sem("a_kT")
        a_in = [sem(f"a_in{i}") for i in range(2)]
        a_qsq = sem("a_qsq")
        a_qms = sem("a_qms")
        a_qrt = sem("a_qrt")
        a_qn = sem("a_qn")
        a_qtr = sem("a_qtr")
        a_qT = sem("a_qT")
        a_dm = sem("a_dm")
        a_bias = sem("a_bias")
        a_s = sem("a_s")
        a_sm = sem("a_sm")
        a_max = sem("a_max")
        a_p = sem("a_p")
        a_pt = sem("a_pt")
        a_pta = sem("a_pta")
        a_ptv = sem("a_ptv")
        a_o = sem("a_o")
        a_oT = sem("a_oT")
        a_ya = sem("a_ya")
        a_yas = sem("a_yas")
        a_rs = sem("a_rs")
        a_yt = sem("a_yt")
        a_mix = sem("a_mix")
        NK = [qb + 1 for qb in range(NT)]
        GA = [A_HEADS * qb for qb in range(NT + 1)]
        GV = [A_HEADS * sum(1 for x in range(qb) if NK[x] > 4) for qb in range(NT + 1)]

        def attention_sp(sp):
            for i in range(2):
                sp.wait_ge(aq_out[i], 16 * NT)
            for qb in range(NT):
                if qb == 0:
                    sp.wait_ge(d_mix, NT)
                if qb >= 2:
                    sp.wait_ge(a_qtr, 2 * (qb - 1))
                sp.dma_start(aqt[qb % 2], aq_dram[qb * P:(qb + 1) * P, :].rearrange("p (h n) -> p h n", h=A_HEADS)
                             ).then_inc(a_in[qb % 2], 16)

        def attention_pool(pool, step):
            pool.wait_ge(topk_done, len(QBS) + 1)
            pool.wait_ge(d_mix, NT)
            for qb in range(NT):
                n = P * NK[qb]
                if qb:
                    pool.wait_ge(a_bias, A_HEADS * qb)
                pool.tensor_tensor(dm[:, 0:n], mask[:, MOFF[qb]:MOFF[qb + 1]], dist[:, S - n:S],
                                   ALU.add).then_inc(a_dm, 1)
                pool.wait_ge(a_dm, qb + 1)
                for h in range(A_HEADS):
                    i = A_HEADS * qb + h
                    if i >= 2:
                        pool.wait_ge(a_sm, i - 1)
                    pool.tensor_scalar(bias[i % 2][:, 0:n], dm[:, 0:n], SLOPES[h], None,
                                       ALU.mult).then_inc(a_bias, 1)

        def attention_act(act):
            for t in range(NT):
                if t:
                    act.wait_ge(a_ksq, t)
                act.activation(sq_junk, small[:, t, 0:A_LAT], ACT.Square, accum_out=kst[:, 0, t:t + 1]
                               ).then_inc(a_ksq, 1)
            act.wait_ge(a_kms, 1)
            act.activation(kst[:, 2, :], kst[:, 1, :], ACT.Sqrt).then_inc(a_krt, 1)
            for i in range(2):
                act.wait_ge(a_ktr, i + 1)
                act.activation(kT[:, i * HALF:(i + 1) * HALF], bank(i), ACT.Copy).then_inc(a_kT, 1)

            def query_squares(qb):
                act.wait_ge(a_in[qb % 2], 16 * (qb // 2 + 1))
                if qb:
                    act.wait_ge(a_qrt, qb)
                for h in range(A_HEADS):
                    act.wait_ge(a_qsq, A_HEADS * qb + h) if qb + h else act.wait_ge(a_ksq, NT)
                    act.activation(sq_junk, aqt[qb % 2][:, h, :], ACT.Square, accum_out=qst[:, 0, h:h + 1]
                                   ).then_inc(a_qsq, 1)

            def query_roots(qb):
                act.wait_ge(a_qms, qb + 1)
                act.activation(qst[:, 2, :], qst[:, 1, :], ACT.Sqrt).then_inc(a_qrt, 1)

            def query_out(qb, i):
                act.wait_ge(a_qtr, 2 * qb + i + 1)
                if qb >= 2:
                    act.wait_ge(a_s, A_HEADS * (qb - 1))
                act.activation(qT[qb % 2][:, 4 * i:4 * i + 4, :], bank(0 if qb == i == 0 else 1).rearrange(
                    "p (h n) -> p h n", h=4), ACT.Copy, scale=qg[:, 0:1]).then_inc(a_qT, 1)

            def take_out(qb, h):
                act.wait_ge(a_pt, GA[qb] + GV[qb] + (2 if NK[qb] > 4 else 1) * h + 1)
                i = A_HEADS * qb + h
                if i >= 4:
                    act.wait_ge(a_o, i // 4)
                w = min(4, NK[qb])
                act.activation(PT[:, 0:w, h % 4, :], bank(6)[:, 0:w * P].rearrange("p (k n) -> p k n", k=w),
                               ACT.Copy).then_inc(a_pta, 1)

            def o_out(qb, g):
                act.wait_ge(a_o, 2 * qb + g + 1)
                if qb:
                    act.wait_ge(a_ya, qb)
                act.activation(oT[:, 4 * g:4 * g + 4, :], bank(g).rearrange("p (h n) -> p h n", h=4),
                               ACT.Copy).then_inc(a_oT, 1)

            def y_out(qb):
                act.wait_ge(a_yt, qb + 1)
                act.activation(mixT[:, 0:4, qb * P:(qb + 1) * P], heads(bank(1)), ACT.Copy).then_inc(a_mix, 1)

            query_squares(0)
            query_roots(0)
            query_out(0, 0)
            query_out(0, 1)
            for qb in range(NT):
                n = P * NK[qb]
                ahead = qb + 1 < NT
                for h in range(A_HEADS):
                    i = A_HEADS * qb + h
                    act.wait_ge(a_max, i + 1)
                    if i >= 2:
                        act.wait_ge(a_pt, GA[qb] + GV[qb] + (2 if NK[qb] > 4 else 1) * (h - 1) if h > 1 else
                                    (GA[qb] + GV[qb] - (2 if NK[qb - 1] > 4 else 1) * (1 - h)))
                    if qb and h == 0:
                        act.wait_ge(a_rs, qb)
                    act.activation(pr[i % 2][:, 0:n], sc[i % 2][:, 0:n], ACT.Exp, bias=smax[:, 1, h:h + 1],
                                   accum_out=smax[:, 2, h:h + 1]).then_inc(a_p, 1)
                    if h == 0 and qb:
                        o_out(qb - 1, 1)
                    if h >= 1:
                        take_out(qb, h - 1)
                    if h == 2 and qb:
                        y_out(qb - 1)
                    if h == 1 and ahead:
                        query_squares(qb + 1)
                    if h == 2 and ahead:
                        query_roots(qb + 1)
                    if h == 5:
                        o_out(qb, 0)
                    if h in (5, 7) and ahead:
                        query_out(qb + 1, (h - 5) // 2)
                take_out(qb, A_HEADS - 1)
            o_out(NT - 1, 1)
            y_out(NT - 1)

        def attention_dve(dve, step):
            step(dve.tensor_scalar(qg[:, :], qg[:, :], ATT_SCALE, None, ALU.mult))
            dve.wait_ge(a_ksq, NT)
            dve.tensor_scalar(kst[:, 1, :], kst[:, 0, :], 1.0 / A_LAT, EPS, ALU.mult, ALU.add).then_inc(a_kms, 1)
            dve.wait_ge(a_krt, 1)
            step(dve.reciprocal(kst[:, 3, :], kst[:, 2, :]))
            for t in range(NT):
                dve.scalar_tensor_tensor(out=ktok[:, t, :], in0=small[:, t, 0:A_LAT], scalar=kst[:, 3, t:t + 1],
                                         in1=kg[:, :], op0=ALU.mult, op1=ALU.mult).then_inc(a_k, 1)

            def query_norm(qb):
                dve.wait_ge(a_qsq, A_HEADS * (qb + 1))
                dve.tensor_scalar(qst[:, 1, :], qst[:, 0, :], 1.0 / A_LAT, EPS, ALU.mult, ALU.add).then_inc(a_qms, 1)

            def query_scale(qb):
                dve.wait_ge(a_qrt, qb + 1)
                step(dve.reciprocal(qst[:, 3, :], qst[:, 2, :]))
                dve.tensor_tensor(aqt[qb % 2], aqt[qb % 2],
                                  qst[:, 3, :].unsqueeze(2).broadcast_to([P, A_HEADS, A_LAT]), ALU.mult
                                  ).then_inc(a_qn, 1)

            def y_scale(qb):
                dve.wait_ge(a_ya, qb + 1)
                dve.wait_ge(a_rs, qb + 1)
                if qb:
                    dve.wait_ge(a_yt, qb)
                dve.tensor_tensor(ya.rearrange("p (h n) -> p h n", h=A_HEADS),
                                  bank(0).rearrange("p (h n) -> p h n", h=A_HEADS),
                                  inv_sum.unsqueeze(2).broadcast_to([P, A_HEADS, A_VDIM]), ALU.mult
                                  ).then_inc(a_yas, 1)

            query_norm(0)
            query_scale(0)
            for qb in range(NT):
                n = P * NK[qb]
                ahead = qb + 1 < NT
                for h in range(A_HEADS):
                    i = A_HEADS * qb + h
                    dve.wait_ge(a_s, i + 1)
                    dve.wait_ge(a_bias, i + 1)
                    if i >= 2:
                        dve.wait_ge(a_p, i - 1)
                    dve.tensor_tensor_reduce(out=sc[i % 2][:, 0:n], in0=bias[i % 2][:, 0:n],
                                             in1=pair[1 + i % 2][:, 0:n], scale=1.0, scalar=TAKEN, op0=ALU.add,
                                             op1=ALU.max, accum_out=smax[:, 0, h:h + 1]).then_inc(a_sm, 1)
                    dve.wait_ge(a_sm, i + 1)
                    dve.tensor_scalar(smax[:, 1, h:h + 1], smax[:, 0, h:h + 1], -1.0, None,
                                      ALU.mult).then_inc(a_max, 1)
                    if NK[qb] > 4 and h:
                        rest_out(dve, qb, h - 1)
                    if h == 1 and qb:
                        y_scale(qb - 1)
                    if h == 2 and ahead:
                        query_norm(qb + 1)
                    if h == 3 and ahead:
                        query_scale(qb + 1)
                if NK[qb] > 4:
                    rest_out(dve, qb, A_HEADS - 1)
                dve.wait_ge(a_p, A_HEADS * (qb + 1))
                if qb:
                    dve.wait_ge(a_yas, qb)
                dve.reciprocal(inv_sum, smax[:, 2, :]).then_inc(a_rs, 1)
            y_scale(NT - 1)

        def rest_out(dve, qb, h):
            i = A_HEADS * qb + h
            dve.wait_ge(a_pt, GA[qb] + GV[qb] + 2 * h + 2)
            dve.wait_ge(a_o, i // 4)
            w = NK[qb] - 4
            dve.tensor_copy(PT[:, 4:4 + w, h % 4, :], bank(7)[:, 0:w * P].rearrange("p (k n) -> p k n", k=w)
                            ).then_inc(a_ptv, 1)

        def attention_pe(pe):
            pe.wait_ge(a_k, NT)
            pe.wait_ge(d_mix, NT)
            for i in range(2):
                for q in range(4):
                    ins = pe.transpose(bank(i)[:, q * P:(q + 1) * P], ktok[:, 4 * i + q, :], ident[:, :])
                ins.then_inc(a_ktr, 1)

            def queries(qb, i):
                pe.wait_ge(a_qn, qb + 1)
                if qb == 0:
                    pe.wait_ge(a_kT, 2)
                elif i == 0:
                    if qb >= 2:
                        pe.wait_ge(a_mix, qb - 1)
                    else:
                        pe.wait_ge(a_qT, 2)
                else:
                    pe.wait_ge(a_qT, 2 * qb + 1)
                for q in range(4):
                    ins = pe.transpose(bank(0 if qb == i == 0 else 1)[:, q * P:(q + 1) * P],
                                       aqt[qb % 2][:, 4 * i + q, :], ident[:, :])
                ins.then_inc(a_qtr, 1)

            def scores(qb, h):
                if h >= A_HEADS:
                    qb, h = qb + 1, h - A_HEADS
                    if qb == NT:
                        return
                n = P * NK[qb]
                i = A_HEADS * qb + h
                pe.wait_ge(a_qT, 2 * qb + h // 4 + 1)
                if i >= 2:
                    pe.wait_ge(a_sm, i - 1)
                for c0 in range(0, n, HALF):
                    w = min(HALF, n - c0)
                    ins = pe.matmul(pair[1 + i % 2][:, c0:c0 + w], qT[qb % 2][:, h, :], kT[:, c0:c0 + w], start=True,
                                    stop=True)
                ins.then_inc(a_s, 1)

            def turn(qb, h):
                i = A_HEADS * qb + h
                pe.wait_ge(a_p, i + 1)
                for g0 in range(0, NK[qb], 4):
                    w = min(4, NK[qb] - g0)
                    if g0:
                        if GV[qb] + h:
                            pe.wait_ge(a_ptv, GV[qb] + h)
                    elif i:
                        pe.wait_ge(a_pta, i)
                    for q in range(w):
                        ins = pe.transpose(bank(6 + g0 // 4)[:, q * P:(q + 1) * P],
                                           pr[i % 2][:, (g0 + q) * P:(g0 + q + 1) * P], ident[:, :])
                    ins.then_inc(a_pt, 1)

            def values(qb, g):
                pe.wait_ge(a_pta, GA[qb] + 4 * g + 4)
                if NK[qb] > 4:
                    pe.wait_ge(a_ptv, GV[qb] + 4 * g + 4)
                if g:
                    pe.wait_ge(a_qT, min(2 * qb + 4, 2 * NT))
                for k in range(NK[qb]):
                    ins = pe.matmul(bank(g), ktok[:, k, :], PT[:, k, :, :], start=(k == 0), stop=(k == NK[qb] - 1))
                ins.then_inc(a_o, 1)

            def up(qb):
                pe.wait_ge(a_oT, 2 * qb + 2)
                for h in range(A_HEADS):
                    ins = pe.matmul(bank(0)[:, h * A_VDIM:(h + 1) * A_VDIM], oT[:, h, :], wuv[:, h, :], start=True,
                                    stop=True)
                ins.then_inc(a_ya, 1)

            def y_turn(qb):
                pe.wait_ge(a_yas, qb + 1)
                for q in range(4):
                    ins = pe.transpose(bank(1)[:, q * P:(q + 1) * P], ya[:, q * P:(q + 1) * P], ident[:, :])
                ins.then_inc(a_yt, 1)

            queries(0, 0)
            queries(0, 1)
            scores(0, 0)
            scores(0, 1)
            for qb in range(NT):
                for h in range(A_HEADS):
                    scores(qb, h + 2)
                    turn(qb, h)
                    if h == 0 and qb:
                        up(qb - 1)
                    if h == 1 and qb:
                        y_turn(qb - 1)
                    if h == 3:
                        values(qb, 0)
                    if h in (4, 6) and qb + 1 < NT:
                        queries(qb + 1, (h - 4) // 2)
                values(qb, 1)
            up(NT - 1)
            y_turn(NT - 1)

        bg_in = sem("bg_in")
        gate_row = sem("gate_row")
        x1_mul = sem("x1_mul")
        x1_done = sem("x1_done")
        x1_out = [sem(f"x1_out{i}") for i in range(2)]
        x1_spill = x1_dram.rearrange("(t p) d -> p t d", p=P)

        def residual_sp(sp):
            sp.wait_ge(a_mix, NT)
            sp.dma_start(xbuf[:, :, :], x_tiles).then_inc(x2_in, 16)
            sp.dma_start(sub[:, :, :], subT).then_inc(sub_in, 16)
            sp.dma_start(bg[:, :, :], b_gate.unsqueeze(0).broadcast_to([P, 2, D])).then_inc(bg_in, 16)

        def spill_sp(sp, hf):
            sp.wait_ge(x1_done, 12 + 4 * hf)
            sp.dma_start(x1_spill[:, 4 * hf:4 * hf + 4, :], xbuf[:, 4 * hf:4 * hf + 4, :]).then_inc(x1_out[hf], 16)

        def gate_row_pe(pe, name, n0):
            for i in range(2):
                w = weights(pe, seg0[name] + i)
                for kc in range(KC):
                    ins = pe.matmul(bank(4 + i), c_rep[:, kc, :], w[:, kc, :], start=(kc == 0), stop=(kc == KC - 1))
                ins.then_inc(ada_mm, 1)

        def gate_row_dve(dve, which, row, n0):
            for i in range(2):
                dve.wait_ge(ada_mm, n0 + i + 1)
                dve.tensor_tensor(row[:, i * HALF:(i + 1) * HALF], bank(4 + i), bg[:, which, i * HALF:(i + 1) * HALF],
                                  ALU.add).then_inc(gate_row, 1)

        def residual_pe(pe):
            pe.wait_ge(a_mix, NT)
            gate_row_pe(pe, "gate1", 4)
            for hf in range(2):
                w = weights(pe, seg0["out"] + hf)
                for t in range(NT):
                    n = hf * NT + t
                    if n >= 4:
                        pe.wait_ge(x1_mul, n - 3)
                    for kc in range(KC):
                        ins = pe.matmul(bank(n % 4), mixT[:, kc, t * P:(t + 1) * P], w[:, kc, :], start=(kc == 0),
                                        stop=(kc == KC - 1))
                    ins.then_inc(out_mm, 1)
            pe.wait_ge(gate_row, 2)
            ada_cols_pe(pe, 2, "scale2", 6)
            ada_cols_pe(pe, 3, "shift2", 8)
            xnorm_pe(pe, 1)

        def residual_dve(dve, step):
            dve.wait_ge(a_mix, NT)
            dve.wait_ge(bg_in, 16)
            gate_row_dve(dve, 0, grow1, 4)
            dve.wait_ge(gate_row, 2)
            dve.wait_ge(x2_in, 16)
            for hf in range(2):
                c0 = hf * HALF
                for t in range(NT):
                    n = hf * NT + t
                    dve.wait_ge(out_mm, n + 1)
                    if n >= 2:
                        dve.wait_ge(x1_done, n - 1)
                    dve.tensor_tensor(gmix[n % 2], bank(n % 4), grow1[:, c0:c0 + HALF], ALU.mult).then_inc(x1_mul, 1)
                    dve.wait_ge(x1_mul, n + 1)
                    dve.tensor_tensor(xbuf[:, t, c0:c0 + HALF], xbuf[:, t, c0:c0 + HALF], gmix[n % 2],
                                      ALU.add).then_inc(x1_done, 1)
            xnorm_dve(dve, 1, step)
            ada_cols_dve(dve, 2, 4, 6)
            ada_cols_dve(dve, 3, 3, 8)
            modulate_dve(dve, 1)

        sub_in = sem("sub_in")
        q_out = sem("q_out")
        s_mm = sem("s_mm")
        s_out = sem("s_out")
        s_top = sem("s_top")
        c_max = sem("c_max")
        c_exp = sem("c_exp")
        c_sel = sem("c_sel")
        c_tr = sem("c_tr")
        c_T = sem("c_T")

        def search_pe(pe):
            def key_scores(g, t):
                n = NT * g + t
                pe.wait_ge(q_out, 8 * g + 8)
                pe.wait_ge(sub_in, 16)
                if n >= 2:
                    pe.wait_ge(s_out, n - 1)
                else:
                    pe.wait_ge(mods_done, 4)
                for j in range(4):
                    ins = pe.matmul(bank(6 + n % 2)[:, j * NKEYS:(j + 1) * NKEYS],
                                    pqT[g % 2][:, j, t * P:(t + 1) * P], sub[:, 4 * g + j, :], start=True, stop=True)
                ins.then_inc(s_mm, 1)

            for g in range(4):
                w = weights(pe, seg0["query"] + g)
                for n8 in range(8):
                    n = 8 * g + n8
                    if n == 0:
                        pe.wait_ge(hx_act, 16)
                        pe.wait_ge(hx_dve, 16)
                    if n >= 4:
                        pe.wait_ge(q_out, n - 3)
                    j, hf = n8 // 2, n8 % 2
                    for kc in range(KC):
                        ins = pe.matmul(bank(n % 4), w[:, kc, j * P:(j + 1) * P], h2T[:, kc, hf * HALF:(hf + 1) * HALF],
                                        start=(kc == 0), stop=(kc == KC - 1))
                    ins.then_inc(q_mm, 1)
                    if g:
                        key_scores(g - 1, n8)
            gate_row_pe(pe, "gate2", 10)
            for t in range(NT):
                key_scores(3, t)
            pe.wait_ge(h_lo_done, KC)
            pe.wait_ge(gate_row, 4)
            for t in range(NT):
                for k in range(PER_TILE):
                    unit_pe(pe, PER_TILE * t + k, k % 4)
                pe.wait_ge(c_sel, t + 1)
                if t >= 2:
                    pe.wait_ge(c_T, t - 1)
                for i in range(3):
                    ins = pe.transpose(bank(t % 2)[:, i * P:(i + 1) * P], sel[t % 2][:, i, :], ident[:, :])
                ins.then_inc(c_tr, 1)

        def search_act(act):
            split_h_act(act)
            def scores_out(n):
                act.wait_ge(s_mm, n + 1)
                if n >= 2:
                    act.wait_ge(s_top, n - 1)
                act.activation(s_st[n % 2], bank(6 + n % 2), ACT.Copy).then_inc(s_out, 1)

            for n in range(32):
                g, j, hf = n // 8, n % 8 // 2, n % 2
                act.wait_ge(q_mm, n + 1)
                if g >= 2:
                    act.wait_ge(s_mm, NT * (g - 1))
                act.activation(pqT[g % 2][:, j, hf * HALF:(hf + 1) * HALF], bank(n % 4), ACT.Copy).then_inc(q_out, 1)
                if g:
                    scores_out(n - 8)
            for n in range(24, 32):
                scores_out(n)
            act.wait_ge(q_mm, 32)
            unit_hi(act, 0, 0)
            for t in range(NT):
                for k in range(PER_TILE):
                    n = PER_TILE * t + k
                    unit_hi(act, n + 1, (k + 1) % 4)
                    if k < PER_TILE - 1:
                        unit_gelu(act, n, k % 4)
                act.wait_ge(c_max, t + 1)
                act.activation(ce, ce, ACT.Exp).then_inc(c_exp, 1)
                unit_gelu(act, n, k % 4)
                act.wait_ge(c_tr, t + 1)
                act.activation(selT[:, 0:3, t * P:(t + 1) * P], bank(t % 2)[:, 0:3 * P].rearrange("p (a n) -> p a n", a=3),
                               ACT.Copy).then_inc(c_T, 1)

        def search_dve(dve, step):
            split_h_dve(dve)
            for g in range(4):
                for t in range(NT):
                    n = NT * g + t
                    dve.wait_ge(s_out, n + 1)
                    s_ = s_st[n % 2]
                    for j in range(4):
                        hp = 4 * g + j
                        row = s_[:, j * NKEYS:(j + 1) * NKEYS]
                        lo, hi = sh[:, t, hp, 0:8], sh[:, t, hp, 8:16]
                        ix = m_ix[:, j * PEER_TOPK:(j + 1) * PEER_TOPK]
                        step(dve.max(lo, row))
                        step(dve.max_index(ix[:, 0:8], lo, row))
                        step(dve.match_replace(out=s_tmp, in_to_replace=lo, in_values=row, imm_value=TAKEN))
                        step(dve.max(hi, s_tmp))
                        step(dve.max_index(ix[:, 8:16], hi, s_tmp))
                    dve.tensor_copy(ih[:, t, 4 * g:4 * g + 4, :], m_ix.rearrange("p (a k) -> p a k", a=4)
                                    ).then_inc(s_top, 1)
                    dve.wait_ge(s_top, n + 1)
            gate_row_dve(dve, 1, grow2, 10)
            K4 = [P, PEER_HEADS, PEER_TOPK, PEER_TOPK]
            K3 = [P, PEER_HEADS, PEER_TOPK]

            def by_head(v):
                return v.rearrange("p (h k) -> p h k", h=PEER_HEADS)

            def pick(dst, at, ids):
                step(dve.tensor_tensor(eq, by_head(at).unsqueeze(3).broadcast_to(K4),
                                       iota_c[:, 0:PEER_TOPK].unsqueeze(1).unsqueeze(1).broadcast_to(K4),
                                       ALU.is_equal))
                step(dve.tensor_tensor(eq, eq, ids.unsqueeze(2).broadcast_to(K4), ALU.mult))
                step(dve.tensor_reduce(by_head(dst), eq, AX.X, ALU.add))

            for t in range(NT):
                tab = sh[:, t, :, :].rearrange("p (h x) k -> p h x k", x=2)
                itab = ih[:, t, :, :].rearrange("p (h x) k -> p h x k", x=2)
                step(dve.tensor_tensor(cand.rearrange("p h (a b) -> p h a b", a=PEER_TOPK),
                                       tab[:, :, 0, :].unsqueeze(3).broadcast_to(K4),
                                       tab[:, :, 1, :].unsqueeze(2).broadcast_to(K4), ALU.add))
                for h in range(PEER_HEADS):
                    row = cand[:, h, :]
                    lo, hi = cs[:, h, 0:8], cs[:, h, 8:16]
                    ix = ci[:, h * PEER_TOPK:(h + 1) * PEER_TOPK]
                    step(dve.max(lo, row))
                    step(dve.max_index(ix[:, 0:8], lo, row))
                    step(dve.match_replace(out=cand2, in_to_replace=lo, in_values=row, imm_value=TAKEN))
                    step(dve.max(hi, cand2))
                    step(dve.max_index(ix[:, 8:16], hi, cand2))
                    unit_lo(dve, PER_TILE * t + h, h % 4)
                step(dve.tensor_tensor(ce, cs, cs[:, :, 0:1].broadcast_to(K3), ALU.subtract))
                step(dve.tensor_scalar(cab[:, 0, :], ci, 4, None, ALU.logical_shift_right))
                step(dve.tensor_scalar(cab[:, 1, :], ci, PEER_TOPK - 1, None, ALU.bitwise_and))
                dve.tensor_copy(cabf[:, :, :], cab[:, :, :]).then_inc(c_max, 1)
                dve.wait_ge(c_max, t + 1)
                if t >= 2:
                    dve.wait_ge(c_tr, t - 1)
                for x in range(2):
                    pick(sel[t % 2][:, x, :], cabf[:, x, :], itab[:, :, x, :])
                dve.wait_ge(c_exp, t + 1)
                step(dve.tensor_reduce(gs, ce, AX.X, ALU.add))
                step(dve.reciprocal(gs, gs))
                dve.tensor_tensor(by_head(sel[t % 2][:, 2, :]), ce, gs.unsqueeze(2).broadcast_to(K3), ALU.mult
                                  ).then_inc(c_sel, 1)
                dve.wait_ge(c_sel, t + 1)

        h_hi_done = sem("h_hi_done")
        h_lo_done = sem("h_lo_done")
        u_in = [sem(f"u_in{j}") for j in range(4)]
        u_hi = sem("u_hi")
        u_lo = sem("u_lo")
        e_mm = sem("e_mm")
        e_act = sem("e_act")
        e_out = [sem(f"e_out{i}") for i in range(2)]
        U_SEARCH = 64
        PER_TILE = U_SEARCH // NT

        def split_h_act(act):
            act.wait_ge(hx_act, 16)
            act.wait_ge(hx_dve, 16)
            act.wait_ge(hx_mm, 32)
            for kc in range(KC):
                act.activation(h_hi[:, kc, :], h2T[:, kc, :], ACT.Copy, scale=SCALE_H).then_inc(h_hi_done, 1)

        def split_h_dve(dve):
            for kc in range(KC):
                dve.wait_ge(h_hi_done, kc + 1)
                dve.scalar_tensor_tensor(out=h_lo[:, kc, :], in0=h2T[:, kc, :], scalar=SCALE_H,
                                         in1=h_hi[:, kc, :], op0=ALU.mult, op1=ALU.subtract).then_inc(h_lo_done, 1)

        def unit_hi(act, n, k):
            act.wait_ge(u_in[k], (n + (4 - k)) * 4)
            if not (isinstance(n, int) and n < 2):
                act.wait_ge(e_mm, n + (-1))
            act.activation(u_split[k % 2][:, 0, :, :], u_raw[k], ACT.Copy, scale=SCALE_U).then_inc(u_hi, 1)

        def unit_lo(dve, n, k):
            dve.wait_ge(u_hi, n + 1)
            dve.scalar_tensor_tensor(out=u_split[k % 2][:, 1, :, :], in0=u_raw[k], scalar=SCALE_U,
                                     in1=u_split[k % 2][:, 0, :, :], op0=ALU.mult, op1=ALU.subtract
                                     ).then_inc(u_lo, 1)

        def unit_pe(pe, n, k):
            pe.wait_ge(u_lo, n + 1)
            if not (isinstance(n, int) and n < 2):
                pe.wait_ge(e_act, n + (-1))
            for kc in range(KC):
                for i, (a, b) in enumerate(((0, h_hi), (0, h_lo), (1, h_hi))):
                    for hf in range(2):
                        ins = pe.matmul(pair[2 + k % 2][:, hf * HALF:(hf + 1) * HALF], u_split[k % 2][:, a, kc, :],
                                        b[:, kc, hf * HALF:(hf + 1) * HALF], start=(kc == 0 and i == 0),
                                        stop=(kc == KC - 1 and i == 2))
            ins.then_inc(e_mm, 1)

        def unit_gelu(act, n, k):
            act.wait_ge(e_mm, n + 1)
            if not (isinstance(n, int) and n < 2):
                act.wait_ge(e_out[k % 2], (n + (-(k % 2))) * 8)
            act.activation(e_stage[k % 2], pair[2 + k % 2][:, :], ACT.Gelu, scale=1.0 / (SCALE_U * SCALE_H)
                           ).then_inc(e_act, 1)

        def unit_load(sp, n, k):
            if not (isinstance(n, int) and n < 4):
                sp.wait_ge(u_lo, n + (-3))
            sp.dma_start(u_raw[k], uT[bass.ds(n, 1), :, :, :].rearrange("o p k n -> p (o k) n")
                         ).then_inc(u_in[k], 16)

        def unit_store(sp, n, k):
            sp.wait_ge(e_act, n + 1)
            sp.dma_start(e_dram[bass.ds(n, 1), :, :].rearrange("o p t -> p (o t)"), e_stage[k % 2]
                         ).then_inc(e_out[k % 2], 16)

        def units_sp(sp):
            sp.wait_ge(q_mm, 32)
            for n in range(4):
                unit_load(sp, n, n)
            with sp.Fori(0, U_SEARCH // 4) as m:
                for k in range(4):
                    unit_load(sp, m * 4 + (k + 4), k)
                    unit_store(sp, m * 4 + k, k)

        oh_ready = sem("oh_ready")
        g_mm = sem("g_mm")
        g_ev = sem("g_ev")
        g_out = [sem(f"g_out{i}") for i in range(2)]
        e_in = [sem(f"e_in{j}") for j in range(SG)]
        v_in = [sem(f"v_in{j}") for j in range(SG)]
        STEP_TOK = 16
        STEPS_N = S // STEP_TOK
        assert STEPS_N == NKEYS - U_SEARCH and G_TOK == 4 * STEP_TOK

        def gates_dve(dve, step):
            dve.wait_ge(c_T, NT)
            step(dve.tensor_scalar(g_hi, selT[:, 2, :], SCALE_G, None, ALU.mult))
            step(dve.scalar_tensor_tensor(out=selT[:, 3, :], in0=selT[:, 2, :], scalar=SCALE_G, in1=g_hi,
                                          op0=ALU.mult, op1=ALU.subtract))
            step(dve.tensor_copy(selT[:, 2, :], g_hi))

            def step_dve(m, k, ahead=True):
                for b in range(4):
                    if b == 2 and ahead:
                        unit_lo(dve, m * 4 + (U_SEARCH + k + 1), (k + 1) % 4)
                    dve.wait_ge(g_mm, m * 16 + (4 * k + b + 1))
                    t0 = m * (4 * STEP_TOK) + (k * STEP_TOK + 4 * b)
                    both = oh[:, b, :].rearrange("p (a t n) -> p a t n", a=2, t=4)
                    step(dve.tensor_tensor(both, iota_c[:, :].unsqueeze(1).unsqueeze(1).broadcast_to([P, 2, 4, P]),
                                           selT[:, 0:2, bass.ds(t0, 4)].unsqueeze(3).broadcast_to([P, 2, 4, P]),
                                           ALU.is_equal))
                    ins = dve.tensor_tensor(oh2[:, 4 * b:4 * b + 4, :, :],
                                            both[:, 1, :, :].unsqueeze(2).broadcast_to([P, 4, 2, P]),
                                            selT[:, 2:4, bass.ds(t0, 4)].rearrange("p i t -> p t i").unsqueeze(3)
                                            .broadcast_to([P, 4, 2, P]), ALU.mult)
                    ins.then_inc(oh_ready, 1)

            unit_lo(dve, U_SEARCH, 0)
            with dve.Fori(0, STEPS_N // 4 - 1) as m:
                step.enter(m, 16)
                for k in range(4):
                    step_dve(m, k)
            step.leave(STEPS_N // 4 - 1)
            for k in range(4):
                step_dve(STEPS_N // 4 - 1, k, k < 3)

        def gates_pe(pe):
            pe.sem_inc(g_mm, 4)
            with pe.Fori(0, STEPS_N // 4) as m:
                for k in range(4):
                    unit_pe(pe, m * 4 + (U_SEARCH + k), k)
                    for b in range(4):
                        c = m * 16 + (4 * k + b + 1)
                        pe.wait_ge(oh_ready, c)
                        pe.wait_ge(g_ev, c)
                        for q in range(4):
                            for i in range(2):
                                ins = pe.matmul(bank(b)[:, q * P:(q + 1) * P], oh[:, b, q * P:(q + 1) * P],
                                                oh2[:, 4 * b + q, i, :], start=(i == 0), stop=(i == 1))
                        ins.then_inc(g_mm, 1)

        def gates_act(act):
            act.wait_ge(c_T, NT)
            act.sem_inc(g_ev, 4)

            def block_out(m, x, first=False, last=False):
                for k in range(4):
                    n = m * 8 + (U_SEARCH + 4 * x + k)
                    if not last or k < 3:
                        unit_hi(act, m * 8 + (U_SEARCH + 4 * x + k + 1), (k + 1) % 4)
                    for b in range(4):
                        act.wait_ge(g_mm, m * 32 + (16 * x + 4 * k + b + 5))
                        if not first and k == 0 and b == 0:
                            act.wait_ge(g_out[x], m * 16)
                        act.activation(gst[x][:, :, STEP_TOK * k + 4 * b:STEP_TOK * k + 4 * b + 4],
                                       bank(b).rearrange("p (t i) -> p i t", t=4), ACT.Copy,
                                       scale=1.0 / SCALE_G).then_inc(g_ev, 1)
                    unit_gelu(act, n, k)

            for x in range(2):
                block_out(0, x, True)
            with act.Fori(1, G_BLOCKS // 2 - 1) as m:
                for x in range(2):
                    block_out(m, x)
            m = G_BLOCKS // 2 - 1
            block_out(m, 0)
            block_out(m, 1, last=True)

        def load_ev(sp, n, j):
            sp.dma_start(e_sb[j], e_dram[bass.ds(n, 1), :, :].rearrange("o p t -> p (o t)")).then_inc(e_in[j], 16)
            sp.dma_start(v_raw[j], v_tab[:, bass.ds(n, 1), :].rearrange("p o d -> p (o d)")).then_inc(v_in[j], 16)

        def gates_sp(sp):
            def step_sp(m, x, k, more):
                if more:
                    unit_load(sp, m * 8 + (U_SEARCH + 4 * x + k + 4), k)
                unit_store(sp, m * 8 + (U_SEARCH + 4 * x + k), k)
                if not more and k == 1:
                    sp.wait_ge(g_out[0], 8 * G_BLOCKS)
                    for i in range(2):
                        sp.wait_ge(e_out[i], 16 * SG // 2)
                    for j in range(SG):
                        load_ev(sp, j, j)
                if k == 3:
                    sp.wait_ge(g_ev, m * 32 + (16 * x + 20))
                    sp.dma_start(g_dram[bass.ds(m * 2 + x, 1), :, :, :].rearrange("b p i t -> p (b i) t"),
                                 gst[x]).then_inc(g_out[x], 16)

            with sp.Fori(0, G_BLOCKS // 2 - 1) as m:
                for x in range(2):
                    for k in range(4):
                        step_sp(m, x, k, True)
            for x in range(2):
                for k in range(4):
                    step_sp(G_BLOCKS // 2 - 1, x, k, x == 0)
            for x in range(2):
                sp.wait_ge(g_out[x], 8 * G_BLOCKS)
                sp.wait_ge(e_out[x], 8 * NKEYS)

        gg_in = [sem(f"gg_in{i}") for i in range(2)]
        e_mul = sem("e_mul")
        a_hi = sem("a_hi")
        a_lo = sem("a_lo")
        v_hi = sem("v_hi")
        v_lo = sem("v_lo")
        y_mm = sem("y_mm")
        y_add = sem("y_add")
        y_fin = sem("y_fin")
        x3_in = sem("x3_in")
        out_out = [sem(f"out_out{i}") for i in range(2)]

        def experts_sp(sp):
            def loads(s, x, i):
                if i == 2:
                    sp.wait_ge(e_mul, s * SG + (-SG))
                sp.dma_start(g_sb[x], g_dram.rearrange("b p i t -> p b i t")[:, :, bass.ds(s * SG, SG), :]
                             ).then_inc(gg_in[x], 16)
                for j in range(SG):
                    if i:
                        sp.wait_ge(a_lo, s * SG + (j + 1 - SG))
                        sp.wait_ge(v_lo, s * SG + (j + 1 - SG))
                        load_ev(sp, s * SG + j, j)
            for s in range(2):
                loads(s, s, s)
            with sp.Fori(1, NSG // 2) as m:
                for x in range(2):
                    loads(m * 2 + x, x, 2)
            sp.wait_ge(a_lo, SG * NSG)
            sp.dma_start(x1_in_sb[:, :, :], x1_spill).then_inc(x3_in, 16)
            out_tiles = out.rearrange("(t p) d -> p t d", p=P)
            for hf in range(2):
                sp.wait_ge(y_fin, 4 * (hf + 1))
                sp.dma_start(out_tiles[:, 4 * hf:4 * hf + 4, :], yacc[:, 4 * hf:4 * hf + 4, :]).then_inc(out_out[hf], 16)
            for hf in range(2):
                sp.wait_ge(out_out[hf], 16)

        def experts_pe(pe):
            pe.wait_ge(e_act, NKEYS)
            pe.wait_ge(g_ev, 4 * STEPS_N + 4)
            with pe.Fori(0, NSG // 2) as m:
                for x in range(2):
                    pe.wait_ge(v_lo, m * (2 * SG) + (SG * x + SG))
                    pe.wait_ge(a_lo, m * (2 * SG) + (SG * x + SG))
                    for q in range(16):
                        t, hf = q // 2, q % 2
                        pe.wait_ge(y_add, m * 32 + (16 * x + q + 1))
                        for k in range(SG):
                            for i, (a, b) in enumerate(((0, 0), (0, 1), (1, 0))):
                                ins = pe.matmul(bank(q % 8), a_split[x][:, k, a, t * P:(t + 1) * P],
                                                v_split[x][:, k, b, hf * HALF:(hf + 1) * HALF],
                                                start=(k == 0 and i == 0), stop=(k == SG - 1 and i == 2))
                        ins.then_inc(y_mm, 1)

        def experts_act(act):
            def split(s, x, first):
                for j in range(SG):
                    act.wait_ge(v_in[j], s * 16 + 16)
                    if j == 0 and not first:
                        act.wait_ge(y_mm, s * 16 + (-16))
                    act.activation(v_split[x][:, j, 0, :], v_raw[j], ACT.Copy, scale=SCALE_V).then_inc(v_hi, 1)
                    act.wait_ge(e_mul, s * SG + (j + 1))
                    act.activation(a_split[x][:, j, 0, :], e_sb[j], ACT.Copy, scale=SCALE_A).then_inc(a_hi, 1)

            for x in range(2):
                split(x, x, True)
            with act.Fori(1, NSG // 2) as m:
                for x in range(2):
                    split(m * 2 + x, x, False)

        def experts_pool(pool, step):
            with pool.Fori(0, NSG // 2) as m:
                for x in range(2):
                    pool.wait_ge(gg_in[x], m * 16 + 16)
                    for j in range(SG):
                        pool.wait_ge(e_in[j], m * 32 + (16 * x + 16))
                        a_ = e_sb[j].rearrange("p (b t) -> p b t", t=G_TOK)
                        pool.tensor_tensor(a_, a_, g_sb[x][:, :, j, :], ALU.mult).then_inc(e_mul, 1)

        def experts_dve(dve, step):
            dve.wait_ge(e_mm, NKEYS)
            step(dve.memset(yacc[:, :, :], 0.0))
            dve.sem_inc(y_add, 8)

            def adds(s, q0):
                for q in range(q0, q0 + 4):
                    t, hf = q // 2, q % 2
                    dve.wait_ge(y_mm, s * 16 + (q + 1))
                    y_ = yacc[:, t, hf * HALF:(hf + 1) * HALF]
                    dve.scalar_tensor_tensor(out=y_, in0=bank(q % 8), scalar=1.0 / (SCALE_A * SCALE_V), in1=y_,
                                             op0=ALU.mult, op1=ALU.add).then_inc(y_add, 1)

            def split(s, x, prev):
                for j in range(SG):
                    dve.wait_ge(v_hi, s * SG + (j + 1))
                    dve.scalar_tensor_tensor(out=v_split[x][:, j, 1, :], in0=v_raw[j], scalar=SCALE_V,
                                             in1=v_split[x][:, j, 0, :], op0=ALU.mult, op1=ALU.subtract
                                             ).then_inc(v_lo, 1)
                    dve.wait_ge(a_hi, s * SG + (j + 1))
                    dve.scalar_tensor_tensor(out=a_split[x][:, j, 1, :], in0=e_sb[j], scalar=SCALE_A,
                                             in1=a_split[x][:, j, 0, :], op0=ALU.mult, op1=ALU.subtract
                                             ).then_inc(a_lo, 1)
                    if prev is not None:
                        adds(prev, 4 * j)

            split(0, 0, None)
            with dve.Fori(0, NSG // 2 - 1) as m:
                split(m * 2 + 1, 1, m * 2)
                split(m * 2 + 2, 0, m * 2 + 1)
            split(NSG - 1, 1, NSG - 2)
            for j in range(SG):
                adds(NSG - 1, 4 * j)
            dve.wait_ge(x3_in, 16)
            dve.wait_ge(y_add, 16 * NSG + 8)
            for t in range(NT):
                step(dve.tensor_tensor(yacc[:, t, :], yacc[:, t, :], grow2, ALU.mult))
                dve.tensor_tensor(yacc[:, t, :], yacc[:, t, :], x1_in_sb[:, t, :], ALU.add).then_inc(y_fin, 1)

        @block.sync
        def _(sp):
            for dst, src in small_loads:
                sp.dma_start(dst, src).then_inc(consts_in, 16)
            def load_weights(first, end):
                for n in range(first, end):
                    if n >= 2:
                        sp.wait_ge(*released[n - 2])
                    for at, src in segs[n]:
                        w = src.shape[2]
                        sp.dma_start(wring[n % 2][:, :, at:at + w], src).then_inc(w_in_s[n % 2], 16)
            load_weights(0, seg0["gate1"])
            sp.wait_ge(d_mix, NT)
            load_weights(seg0["gate1"], seg0["out"])
            attention_sp(sp)
            residual_sp(sp)
            load_weights(seg0["out"], seg0["shift2"])
            spill_sp(sp, 0)
            load_weights(seg0["shift2"], seg0["shift2"] + 1)
            spill_sp(sp, 1)
            load_weights(seg0["shift2"] + 1, NSEG)
            units_sp(sp)
            gates_sp(sp)
            experts_sp(sp)

        @block.gpsimd
        def _(pool):
            step = Steps(pool, pool_const)
            for t_, v in ((ident, 0.0), (ones, 1.0), (triu, 1.0), (causal, 0.0)):
                pool.memset(t_[:, :], v).then_inc(pool_const, 1)
            pool.memset(level[:, :, :], 0.0).then_inc(pool_const, 1)
            pool.memset(eps[:, 0:1], EPS).then_inc(pool_const, 1)
            pool.memset(eps[:, 1:2], EPS * B_DIM).then_inc(pool_const, 1)
            pool.iota(iota_c[:, :], [[1, P]], base=0, channel_multiplier=0,
                      allow_small_or_imprecise_dtypes=True).then_inc(pool_const, 1)
            pool.iota(dist[:, :], [[1, S]], base=-(S - P), channel_multiplier=-1,
                      allow_small_or_imprecise_dtypes=True).then_inc(pool_const, 1)
            step.n = 9
            pool.wait_ge(pool_const, 9)
            step(pool.affine_select(out=ident[:, :], in_=ident[:, :], compare_op=ALU.not_equal, fill=1.0, base=0,
                                    pattern=[[-1, P]], channel_multiplier=1))
            step(pool.affine_select(out=triu[:, :], in_=triu[:, :], compare_op=ALU.is_ge, fill=0.0, base=0,
                                    pattern=[[1, P]], channel_multiplier=-1))
            step(pool.affine_select(out=causal[:, :], in_=causal[:, :], compare_op=ALU.is_ge, fill=MASKED, base=0,
                                    pattern=[[-1, P]], channel_multiplier=1))
            for l in range(LEVELS):
                s_, nb = 2 ** l, P >> (l + 1)
                v = level[:, l, :].rearrange("p (b x s) -> p b x s", b=nb, x=2)[:, :, 1, :]
                step(pool.memset(v, 1.0))
                step(pool.affine_select(out=v, in_=v, compare_op=ALU.is_ge, fill=0.0, base=0,
                                        pattern=[[-2 * s_, nb], [0, s_]], channel_multiplier=1))
                step(pool.affine_select(out=v, in_=v, compare_op=ALU.is_ge, fill=0.0, base=s_ - 1,
                                        pattern=[[2 * s_, nb], [0, s_]], channel_multiplier=-1))
            assert step.n == POOL_CONSTS
            step = Steps(pool, pool_c)
            pool.wait_ge(proj_out, N_SMALL)
            pool.memset(raw[:, :, 0:CONV_W - 1], 0.0).then_inc(raw_pad, 1)
            step(pool.tensor_scalar(iw_s[:, :, :], small[:, :, 128:132], IDX_SCALE, None, ALU.mult))
            for k, qb in enumerate(QBS):
                n = P * (qb + 1)
                if k >= 2:
                    pool.wait_ge(topk_done, k - 1)
                for h in range(IDX_HEADS):
                    i = k * IDX_HEADS + h
                    pool.wait_ge(idx_relu, i + 1)
                    wcol = iw_s[:, qb, h:h + 1]
                    if h == 0:
                        pool.tensor_scalar(score[k % 2][:, 0:n], relu[i % 2][:, 0:n], wcol, None,
                                           ALU.mult).then_inc(idx_acc, 1)
                    else:
                        pool.wait_ge(idx_acc, i)
                        step(pool.tensor_scalar(weighed[:, 0:n], relu[i % 2][:, 0:n], wcol, None, ALU.mult))
                        pool.tensor_tensor(score[k % 2][:, 0:n], score[k % 2][:, 0:n], weighed[:, 0:n],
                                           ALU.add).then_inc(idx_acc, 1)
                pool.wait_ge(idx_acc, (k + 1) * IDX_HEADS)
                pool.tensor_tensor(score[k % 2][:, n - P:n], score[k % 2][:, n - P:n], causal[:, :],
                                   ALU.add).then_inc(score_done, 1)
            pool.wait_ge(proj_out, len(jobs))
            pool.wait_ge(score_done, len(QBS))
            pool.tensor_copy(late_score, score[(len(QBS) - 1) % 2]).then_inc(late_in, 1)
            delta_pool(pool, step)
            attention_pool(pool, step)
            experts_pool(pool, step)

        def xnorm_act(act, which):
            for hf in range(2):
                if which == 0:
                    act.wait_ge(x_in[hf], 16)
                else:
                    act.wait_ge(x1_done, 12 + 4 * hf)
                for t in range(4 * hf, 4 * hf + 4):
                    if 8 * which + t:
                        act.wait_ge(sq_done, 8 * which + t)
                    act.activation(njunk, xbuf[:, t, :], ACT.Square, accum_out=st[:, 0, 8 * which + t:8 * which + t + 1]
                                   ).then_inc(sq_done, 1)
                act.wait_ge(ms_done, 2 * which + hf + 1)
                o = slice(8 * which + 4 * hf, 8 * which + 4 * hf + 4)
                act.activation(st[:, 2, o], st[:, 1, o], ACT.Sqrt).then_inc(rt_done, 1)
            dst = (hT, h2T)[which]
            for j in range(0, 16, 2):
                hf, kc = j // 8, j % 8
                act.wait_ge(hx_mm, 16 * which + j + 1)
                act.wait_ge(mods_done, 2 * which + 2)
                act.activation(dst[:, kc, hf * HALF:(hf + 1) * HALF], bank(j % 4), ACT.Identity,
                               bias=mods[:, 2 * which + 1, kc:kc + 1],
                               scale=mods[:, 2 * which, kc:kc + 1]).then_inc(hx_act, 1)

        def xnorm_dve(dve, which, step):
            for hf in range(2):
                o = slice(8 * which + 4 * hf, 8 * which + 4 * hf + 4)
                dve.wait_ge(sq_done, 8 * which + 4 * (hf + 1))
                dve.tensor_scalar(st[:, 1, o], st[:, 0, o], 1.0 / D, EPS, ALU.mult, ALU.add).then_inc(ms_done, 1)
                dve.wait_ge(rt_done, 2 * which + hf + 1)
                dve.wait_ge(ms_done, 2 * which + hf + 1)
                step(dve.reciprocal(st[:, 3, o], st[:, 2, o]))
                step(dve.tensor_tensor(st[:, 4, o], st[:, 3, o], st[:, 3, o], ALU.mult))
                step(dve.tensor_tensor(st[:, 4, o], st[:, 4, o], st[:, 1, o], ALU.mult))
                step(dve.tensor_scalar(st[:, 4, o], st[:, 4, o], -0.5, 1.5, ALU.mult, ALU.add))
                step(dve.tensor_tensor(st[:, 5, o], st[:, 4, o], st[:, 3, o], ALU.mult))
                if which:
                    dve.wait_ge(x1_out[hf], 16)
                for t in range(4 * hf, 4 * hf + 4):
                    dve.tensor_scalar(xbuf[:, t, :], xbuf[:, t, :], st[:, 5, 8 * which + t:8 * which + t + 1], None,
                                      ALU.mult).then_inc(xn_done, 1)

        def modulate_dve(dve, which):
            dst = (hT, h2T)[which]
            for j in range(1, 16, 2):
                hf, kc = j // 8, j % 8
                dve.wait_ge(hx_mm, 16 * which + j + 1)
                dve.wait_ge(mods_done, 2 * which + 2)
                dve.tensor_scalar(dst[:, kc, hf * HALF:(hf + 1) * HALF], bank(j % 4),
                                  mods[:, 2 * which, kc:kc + 1], mods[:, 2 * which + 1, kc:kc + 1],
                                  ALU.mult, ALU.add).then_inc(hx_dve, 1)

        def xnorm_pe(pe, which):
            for j in range(16):
                hf, kc = j // 8, j % 8
                pe.wait_ge(xn_done, 8 * which + 4 * hf + 4)
                if j >= 4:
                    pe.wait_ge(hx_dve if j % 2 else hx_act, 8 * which + (j - 4) // 2 + 1)
                for q in range(4):
                    ins = pe.transpose(bank(j % 4)[:, q * P:(q + 1) * P],
                                       xbuf[:, 4 * hf + q, kc * P:(kc + 1) * P], ident[:, :])
                ins.then_inc(hx_mm, 1)

        def ada_cols_pe(pe, m, name, n0):
            for i in range(2):
                w = weights(pe, seg0[name] + i)
                for j in range(4):
                    for kc in range(KC):
                        ins = pe.matmul(bank(6 + m % 2)[:, m * KC + 4 * i + j:m * KC + 4 * i + j + 1],
                                        w[:, kc, j * P:(j + 1) * P], c_sb[:, kc:kc + 1],
                                        start=(kc == 0), stop=(kc == KC - 1))
                ins.then_inc(ada_mm, 1)

        def ada_cols_dve(dve, m, part, n0):
            dve.wait_ge(ada_mm, n0 + 2)
            dve.scalar_tensor_tensor(out=mods[:, m, :], in0=bank(6 + m % 2)[:, m * KC:(m + 1) * KC],
                                     scalar=1.0 if m % 2 == 0 else 0.0, in1=b_sb[:, part * KC:(part + 1) * KC],
                                     op0=ALU.add, op1=ALU.add).then_inc(mods_done, 1)

        njunk = Region(R4 + D).take(D)

        @block.scalar
        def _(act):
            for hf in range(2):
                act.dma_start(xbuf[:, 4 * hf:4 * hf + 4, :], x_tiles[:, 4 * hf:4 * hf + 4, :]).then_inc(x_in[hf], 16)
            act.wait_ge(consts_in, CONSTS)
            act.activation(c_sb[:, :], c_sb[:, :], ACT.Silu).then_inc(silu_c, 1)
            xnorm_act(act, 0)
            act.wait_ge(pool_const, POOL_CONSTS)
            act.wait_ge(hx_mm, 16)

            def index_relus(k):
                qb = QBS[k]
                n = P * (qb + 1)
                for h in range(IDX_HEADS):
                    i = k * IDX_HEADS + h
                    act.wait_ge(idx_mm, i + 1)
                    if i >= 2:
                        act.wait_ge(idx_acc, i - 1)
                    act.activation(relu[i % 2][:, 0:n], pair[2 + i % 2][:, 0:n], ACT.Relu).then_inc(idx_relu, 1)

            for n, (kind, seg, t, h) in enumerate(jobs):
                for k, at in enumerate(IDX_AT):
                    if at == n:
                        index_relus(k)
                act.wait_ge(proj_mm, n + 1)
                b = bank(n % 4)
                if kind == "index":
                    act.activation(iqT[:, t, h * HALF:(h + 1) * HALF], b, ACT.Copy).then_inc(proj_out, 1)
                elif kind == "small":
                    act.activation(small[:, t, :], b[:, 0:140], ACT.Copy).then_inc(proj_out, 1)
                elif kind == "qkv":
                    lo = CONV_W - 1 + h * HALF
                    act.activation(raw[:, t, lo:lo + HALF], b, ACT.Copy).then_inc(proj_out, 1)
                elif kind == "z":
                    act.activation(z[:, t, :], b, ACT.Silu).then_inc(proj_out, 1)
                else:
                    i = n - (len(jobs) - 2 * NT)
                    if i >= 2:
                        act.wait_ge(aq_out[i % 2], 16 * (i // 2))
                    act.activation(aq_stage[i % 2], b, ACT.Copy).then_inc(proj_out, 1)
                    act.wait_ge(proj_out, n + 1)
                    act.dma_start(aq_dram[t * P:(t + 1) * P, h * HALF:(h + 1) * HALF],
                                  aq_stage[i % 2]).then_inc(aq_out[i % 2], 16)
                if SILU_AT <= n < SILU_AT + 12:
                    conv_silu(act, n - SILU_AT)
                if ROOT_AT <= n < ROOT_AT + 2 * H4:
                    l2_root(act, n - ROOT_AT)
            for i in range(2):
                act.wait_ge(aq_out[i], 16 * NT)
            delta_act(act)
            attention_act(act)
            xnorm_act(act, 1)
            search_act(act)
            gates_act(act)
            experts_act(act)

        @block.tensor
        def _(pe):
            pe.wait_ge(pool_const, POOL_CONSTS)
            pe.wait_ge(silu_c, 1)
            ada_cols_pe(pe, 0, "scale1", 0)
            ada_cols_pe(pe, 1, "shift1", 2)
            xnorm_pe(pe, 0)

            def index_logits(k):
                qb = QBS[k]
                n = P * (qb + 1)
                for h in range(IDX_HEADS):
                    i = k * IDX_HEADS + h
                    if i >= 2:
                        pe.wait_ge(idx_relu, i - 1)
                    lo = IDX_DIM * (h % 2)
                    for c0 in range(0, n, HALF):
                        w = min(HALF, n - c0)
                        ins = pe.matmul(pair[2 + i % 2][:, c0:c0 + w],
                                        iqT[lo:lo + IDX_DIM, h // 2, qb * P:(qb + 1) * P],
                                        iqT[lo:lo + IDX_DIM, 2, c0:c0 + w], start=True, stop=True)
                    ins.then_inc(idx_mm, 1)

            pe.wait_ge(hx_act, 8)
            pe.wait_ge(hx_dve, 8)
            for n, (kind, seg, t, h) in enumerate(jobs):
                for k, at in enumerate(IDX_AT):
                    if at == n:
                        if k == 0:
                            pe.wait_ge(proj_out, 6)
                        index_logits(k)
                w = weights(pe, seg)
                if n >= 4:
                    pe.wait_ge(proj_out, n - 3)
                b = bank(n % 4)
                for kc in range(KC):
                    se = {"start": kc == 0, "stop": kc == KC - 1}
                    if kind in ("index", "qkv"):
                        c0 = (t % 4) * P
                        ins = pe.matmul(b, w[:, kc, c0:c0 + P], hT[:, kc, h * HALF:(h + 1) * HALF], **se)
                    else:
                        wd = 140 if kind == "small" else HALF
                        ins = pe.matmul(b[:, 0:wd], hT[:, kc, t * P:(t + 1) * P], w[:, kc, 0:wd], **se)
                ins.then_inc(proj_mm, 1)
                if ROOT_AT + 1 <= n < ROOT_AT + 1 + 2 * H4:
                    l2_sum(pe, n - ROOT_AT - 1)
            delta_pe(pe)
            attention_pe(pe)
            residual_pe(pe)
            search_pe(pe)
            gates_pe(pe)
            experts_pe(pe)

        @block.vector
        def _(dve):
            step = Steps(dve, dve_c)
            dve.wait_ge(silu_c, 1)
            step(dve.tensor_copy(c_rep[:, :, :], c_sb[:, :].unsqueeze(2).broadcast_to([P, KC, P])))
            xnorm_dve(dve, 0, step)
            ada_cols_dve(dve, 0, 1, 0)
            ada_cols_dve(dve, 1, 0, 2)
            modulate_dve(dve, 0)
            for k, qb in enumerate(QBS[:-1]):
                s_ = score[k % 2][:, 0:P * (qb + 1)]
                dve.wait_ge(score_done, k + 1)
                for _ in range(TOPK // 8):
                    topk_round(dve, step, s_, top8)
                topk_mask(dve, qb, s_)
            conv_dve(dve, step)
            dve.wait_ge(pool_const, POOL_CONSTS)
            step(dve.tensor_copy(mask[:, 0:P], causal[:, :]))
            step(dve.memset(mask[:, P:2 * P], 0.0))
            dve.tensor_copy(mask[:, 2 * P:3 * P], causal[:, :]).then_inc(topk_done, 1)
            delta_dve(dve, step)
            attention_dve(dve, step)
            residual_dve(dve, step)
            search_dve(dve, step)
            gates_dve(dve, step)
            experts_dve(dve, step)


_INS = ["x", "c_col", "w_ada", "b_col", "b_gate", "w_in", "q_gain_col", "k_gain", "w_uv", "conv_col", "a_log",
        "dt_bias", "gdn_gain", "w_out", "w_query", "subT", "uT", "v_tab"]


def laid_out(x, c, w_ada, b_ada, w_in, q_gain, k_gain, w_uv, conv_w, a_log, dt_bias, gdn_gain, w_out,
             w_query, sub_keys, u_tab, v_tab):
    def arr(a):
        return np.ascontiguousarray(a)
    return {
        "x": arr(x),
        "c_col": arr(np.asarray(c).reshape(KC, P).T),
        "w_ada": arr(w_ada[0]),
        "b_col": arr(np.asarray(b_ada).reshape(48, P).T),
        "b_gate": arr(np.asarray(b_ada).reshape(6, D)[[2, 5]]),
        "w_in": arr(w_in[0]),
        "q_gain_col": arr(np.asarray(q_gain).reshape(P, 1)),
        "k_gain": arr(k_gain),
        "w_uv": arr(w_uv),
        "conv_col": arr(np.asarray(conv_w).reshape(CONV_W, 12, P).transpose(2, 1, 0)),
        "a_log": arr(a_log),
        "dt_bias": arr(dt_bias),
        "gdn_gain": arr(gdn_gain),
        "w_out": arr(w_out[0]),
        "w_query": arr(w_query[0]),
        "subT": arr(np.asarray(sub_keys).reshape(16, NKEYS, P).transpose(2, 0, 1)),
        "uT": arr(np.asarray(u_tab).reshape(NKEYS, NKEYS, KC, P).transpose(1, 3, 2, 0)),
        "v_tab": arr(np.asarray(v_tab).reshape(NKEYS, NKEYS, D)),
    }


def kernel(x, c, w_ada, b_ada, w_in, q_gain, k_gain, w_uv, conv_w, a_log, dt_bias, gdn_gain, w_out,
           w_query, sub_keys, u_tab, v_tab):
    import concourse.bacc as bacc
    from concourse.bass_utils import run_bass_kernel_spmd

    nc = bacc.Bacc("TRN2", target_bir_lowering=False, num_devices=1)
    data = laid_out(x, c, w_ada, b_ada, w_in, q_gain, k_gain, w_uv, conv_w, a_log, dt_bias, gdn_gain, w_out,
                    w_query, sub_keys, u_tab, v_tab)
    args = [nc.dram_tensor(n, data[n].shape, F32, kind="ExternalInput").ap() for n in _INS]
    out = nc.dram_tensor("out", [S, D], F32, kind="ExternalOutput").ap()
    layer(nc, *args, out)
    r = run_bass_kernel_spmd(nc, [data], core_ids=[0])
    return np.asarray(r.results[0]["out"]).reshape(1, S, D)
```
